# Optimizing a Trainium2 kernel written in Bass

```python
import jax, jax.numpy as jnp
from jax import lax
import numpy as np

D_MODEL = 1024
BATCH = 1
SEQ = 512
DEPTH = 2

N_A_LAYERS = DEPTH // 2
N_B_LAYERS = DEPTH - N_A_LAYERS

M_EXPAND = 2
M_D_INNER = M_EXPAND * D_MODEL
M_HEADDIM = 64
M_HEADS = M_D_INNER // M_HEADDIM
M_GROUPS = 4
M_D_STATE = 128
M_D_CONV = 4
M_CHUNK = 128
M_CONV_DIM = M_D_INNER + 2 * M_GROUPS * M_D_STATE
M_IN_DIM = 2 * M_D_INNER + 2 * M_GROUPS * M_D_STATE + M_HEADS

SB_HEAD_DIM = 64
SB_HEADS = D_MODEL // SB_HEAD_DIM
SB_WIDTH = SB_HEADS * SB_HEAD_DIM
SB_BLOCK = 128

EPS = 1e-6


def _rmsnorm(x, g):
    xf = x.astype(jnp.float32)
    xf = xf * lax.rsqrt(jnp.mean(xf * xf, axis=-1, keepdims=True) + EPS)
    return (xf * g.astype(jnp.float32)).astype(x.dtype)

def _modulate(x, g, shift, scale):
    return _rmsnorm(x, g) * (1.0 + scale[:, None, :]) + shift[:, None, :]

def _causal_dwconv(u, w, b):
    k = w.shape[0]
    out = lax.conv_general_dilated(
        u, w[:, None, :].astype(u.dtype), window_strides=(1,), padding=[(k - 1, 0)],
        dimension_numbers=('NWC', 'WIO', 'NWC'), feature_group_count=u.shape[-1])
    return out + b

def _ssd_chunked(xs, dt, a_neg, bm, cm):
    b, s, h, p = xs.shape
    g, n = bm.shape[2], bm.shape[3]
    hg = h // g
    nc = s // M_CHUNK
    xdt = (xs.astype(jnp.float32) * dt[..., None]).reshape(b, s, g, hg, p)
    a = (dt * a_neg).reshape(b, s, g, hg)

    def chunks(t):
        return jnp.moveaxis(t.reshape((b, nc, M_CHUNK) + t.shape[2:]), 1, 0)

    causal = jnp.tril(jnp.ones((M_CHUNK, M_CHUNK), dtype=bool))[None, :, :, None, None]

    def step(state, inp):
        xc, ac, bc, cc = inp
        acum = jnp.cumsum(ac, axis=1)
        seg = jnp.where(causal, acum[:, :, None] - acum[:, None, :], -jnp.inf)
        scores = jnp.einsum('btgn,bsgn->btsg', cc, bc)[..., None] * jnp.exp(seg)
        y_diag = jnp.einsum('btsgh,bsghp->btghp', scores, xc)
        y_off = jnp.einsum('btgn,bghpn->btghp', cc, state) * jnp.exp(acum)[..., None]
        w_end = jnp.exp(acum[:, -1:] - acum)
        new_state = (state * jnp.exp(acum[:, -1])[..., None, None]
                     + jnp.einsum('bsgn,bsghp->bghpn', bc, xc * w_end[..., None]))
        return new_state, y_diag + y_off

    state0 = jnp.zeros((b, g, hg, p, n), jnp.float32)
    _, ys = lax.scan(step, state0, (chunks(xdt), chunks(a),
                                    chunks(bm.astype(jnp.float32)), chunks(cm.astype(jnp.float32))))
    return jnp.moveaxis(ys, 0, 1).reshape(b, s, h, p)

def _mamba2_mixer(h, in_w, conv_w, conv_b, dt_bias, a_log, d_skip, norm_g, out_w):
    b, s, _ = h.shape
    zxbcdt = h @ in_w
    z = zxbcdt[..., :M_D_INNER]
    xbc = zxbcdt[..., M_D_INNER:M_D_INNER + M_CONV_DIM]
    dt = zxbcdt[..., M_D_INNER + M_CONV_DIM:]
    xbc = jax.nn.silu(_causal_dwconv(xbc, conv_w, conv_b))
    gn = M_GROUPS * M_D_STATE
    xs = xbc[..., :M_D_INNER].reshape(b, s, M_HEADS, M_HEADDIM)
    bm = xbc[..., M_D_INNER:M_D_INNER + gn].reshape(b, s, M_GROUPS, M_D_STATE)
    cm = xbc[..., M_D_INNER + gn:].reshape(b, s, M_GROUPS, M_D_STATE)
    dt = jax.nn.softplus(dt.astype(jnp.float32) + dt_bias.astype(jnp.float32))
    a_neg = -jnp.exp(a_log.astype(jnp.float32))
    y = _ssd_chunked(xs, dt, a_neg, bm, cm)
    y = y + d_skip.astype(jnp.float32)[:, None] * xs.astype(jnp.float32)
    y = y.reshape(b, s, M_D_INNER) * jax.nn.silu(z.astype(jnp.float32))
    yg = y.reshape(b, s, M_GROUPS, M_D_INNER // M_GROUPS)
    yg = yg * lax.rsqrt(jnp.mean(yg * yg, axis=-1, keepdims=True) + EPS)
    y = yg.reshape(b, s, M_D_INNER) * norm_g.astype(jnp.float32)
    return y.astype(h.dtype) @ out_w

def _stick_breaking(q, k, v):
    s_len = q.shape[1]
    scale = SB_HEAD_DIM ** -0.5
    outs = []
    for i in range(s_len // SB_BLOCK):
        lo, hi = i * SB_BLOCK, (i + 1) * SB_BLOCK
        z = jnp.einsum('bthd,bshd->bhts', q[:, lo:hi], k[:, :hi]).astype(jnp.float32) * scale
        mask = ((lo + jnp.arange(SB_BLOCK))[:, None] > jnp.arange(hi)[None, :])[None, None]
        log_keep = jnp.where(mask, jax.nn.log_sigmoid(-z), 0.0)
        after = lax.cumsum(log_keep, axis=3, reverse=True) - log_keep
        log_a = jnp.where(mask, jax.nn.log_sigmoid(z) + after, -jnp.inf)
        a = jnp.exp(log_a).astype(v.dtype)
        outs.append(jnp.einsum('bhts,bshd->bthd', a, v[:, :hi]))
    return jnp.concatenate(outs, axis=1)

def _sb_mixer(h, k, v, in_w, out_w):
    b, s, _ = h.shape
    qz = h @ in_w
    q = qz[..., :SB_WIDTH].reshape(b, s, SB_HEADS, SB_HEAD_DIM)
    z = qz[..., SB_WIDTH:]
    o = _stick_breaking(q, k, v).reshape(b, s, SB_WIDTH)
    return (o * jax.nn.silu(z)) @ out_w

def first_inputs(seed: int = 0) -> dict:
    key = jax.random.key(seed)
    ks = jax.random.split(key, 24)
    f32 = jnp.float32

    def nrm(k, shape, fan_in, mult=1.0):
        return jax.random.normal(k, shape, f32) * (mult * fan_in ** -0.5)

    def gain(k, shape):
        return 1.0 + 0.05 * jax.random.normal(k, shape, f32)

    def small(k, shape):
        return 0.01 * jax.random.normal(k, shape, f32)

    x = jax.random.normal(ks[0], (BATCH, SEQ, D_MODEL), f32)
    c = jax.random.normal(ks[1], (BATCH, D_MODEL), f32)
    ada_w = nrm(ks[2], (DEPTH, D_MODEL, 3 * D_MODEL), D_MODEL, 0.5)
    ada_b = small(ks[3], (DEPTH, 3 * D_MODEL))
    norm_g = gain(ks[4], (DEPTH, D_MODEL))
    m_in_w = nrm(ks[5], (N_A_LAYERS, D_MODEL, M_IN_DIM), D_MODEL)
    m_conv_w = nrm(ks[6], (N_A_LAYERS, M_D_CONV, M_CONV_DIM), M_D_CONV)
    m_conv_b = small(ks[7], (N_A_LAYERS, M_CONV_DIM))
    dt0 = jnp.exp(jax.random.uniform(ks[8], (N_A_LAYERS, M_HEADS), f32,
                                     np.log(1e-3).astype(np.float32), np.log(1e-1).astype(np.float32)))
    m_dt_bias = dt0 + jnp.log(-jnp.expm1(-dt0))
    m_a_log = jnp.log(jax.random.uniform(ks[9], (N_A_LAYERS, M_HEADS), f32, 1.0, 16.0))
    m_d = 1.0 + 0.1 * jax.random.normal(ks[10], (N_A_LAYERS, M_HEADS), f32)
    m_norm_g = gain(ks[11], (N_A_LAYERS, M_D_INNER))
    m_out_w = nrm(ks[12], (N_A_LAYERS, M_D_INNER, D_MODEL), M_D_INNER)
    kv_ada_w = nrm(ks[13], (D_MODEL, 2 * D_MODEL), D_MODEL, 0.5)
    kv_ada_b = small(ks[14], (2 * D_MODEL,))
    kv_norm_g = gain(ks[15], (D_MODEL,))
    kv_w = nrm(ks[16], (D_MODEL, 2 * SB_WIDTH), D_MODEL)
    sb_in_w = nrm(ks[17], (N_B_LAYERS, D_MODEL, 2 * SB_WIDTH), D_MODEL)
    sb_out_w = nrm(ks[18], (N_B_LAYERS, SB_WIDTH, D_MODEL), SB_WIDTH)
    final_g = gain(ks[19], (D_MODEL,))
    return {'x': x, 'c': c, 'ada_w': ada_w, 'ada_b': ada_b, 'norm_g': norm_g,
            'm_in_w': m_in_w, 'm_conv_w': m_conv_w, 'm_conv_b': m_conv_b,
            'm_dt_bias': m_dt_bias, 'm_a_log': m_a_log, 'm_d': m_d,
            'm_norm_g': m_norm_g, 'm_out_w': m_out_w,
            'kv_ada_w': kv_ada_w, 'kv_ada_b': kv_ada_b, 'kv_norm_g': kv_norm_g, 'kv_w': kv_w,
            'sb_in_w': sb_in_w, 'sb_out_w': sb_out_w, 'final_g': final_g}

def first_block(x, c, ada_w, ada_b, norm_g, m_in_w, m_conv_w, m_conv_b, m_dt_bias, m_a_log,
              m_d, m_norm_g, m_out_w, kv_ada_w, kv_ada_b, kv_norm_g, kv_w,
              sb_in_w, sb_out_w, final_g):
    b, s, _ = x.shape
    c_act = jax.nn.silu(c)

    for i in range(N_A_LAYERS):
        shift, scale, gate = jnp.split(c_act @ ada_w[i] + ada_b[i], 3, axis=-1)
        h = _modulate(x, norm_g[i], shift, scale)
        y = _mamba2_mixer(h, m_in_w[i], m_conv_w[i], m_conv_b[i], m_dt_bias[i], m_a_log[i],
                          m_d[i], m_norm_g[i], m_out_w[i])
        x = x + gate[:, None, :] * y

    kv_shift, kv_scale = jnp.split(c_act @ kv_ada_w + kv_ada_b, 2, axis=-1)
    hk = _modulate(x, kv_norm_g, kv_shift, kv_scale)
    kv = hk @ kv_w
    k = kv[..., :SB_WIDTH].reshape(b, s, SB_HEADS, SB_HEAD_DIM)
    v = kv[..., SB_WIDTH:].reshape(b, s, SB_HEADS, SB_HEAD_DIM)

    for j in range(N_B_LAYERS):
        i = N_A_LAYERS + j
        shift, scale, gate = jnp.split(c_act @ ada_w[i] + ada_b[i], 3, axis=-1)
        h = _modulate(x, norm_g[i], shift, scale)
        y = _sb_mixer(h, k, v, sb_in_w[j], sb_out_w[j])
        x = x + gate[:, None, :] * y

    return _rmsnorm(x, final_g)


DEPTH_2 = 1

CHUNK = 64
PLE_DIM = 256
A_HEADS = 4
A_DK = 128
A_DV = 128
A_WIDTH = A_HEADS * A_DV
B_HEADS = 8
B_HD = 64
B_WIDTH = B_HEADS * B_HD
B_LEFT_CHUNKS = 8
B_BAND = (B_LEFT_CHUNKS + 1) * CHUNK
MAX_REL = 128
N_REL = 2 * MAX_REL + 1
D_FF = ((8 * D_MODEL // 3 + 255) // 256) * 256
IN_SIZES = (A_HEADS * A_DK, A_HEADS * A_DK, A_WIDTH, A_WIDTH,
            B_WIDTH, B_WIDTH, B_WIDTH,
            D_MODEL, D_MODEL)
D_IN = sum(IN_SIZES)


def rmsnorm(x, g):
    x32 = x.astype(jnp.float32)
    y = x32 * lax.rsqrt(jnp.mean(x32 * x32, axis=-1, keepdims=True) + EPS)
    return (y * g.astype(jnp.float32)).astype(x.dtype)

def head_rms(t, g):
    t32 = t.astype(jnp.float32)
    return t32 * lax.rsqrt(jnp.mean(t32 * t32, axis=-1, keepdims=True) + EPS) * g.astype(jnp.float32)

def hgrn2_mixer(q, f_logit, i, g, lb, onorm_g):
    f32 = jnp.float32
    bsz, seq, _ = q.shape
    nc = seq // CHUNK
    lb32 = lb.astype(f32)
    logf = jnp.logaddexp(jnp.log(lb32), jnp.log1p(-lb32) + jax.nn.log_sigmoid(f_logit.astype(f32)))
    k = 1.0 - jnp.exp(logf)

    def heads(t, d):
        return t.astype(f32).reshape(bsz, nc, CHUNK, A_HEADS, d).transpose(1, 0, 3, 2, 4)

    qc = heads(q, A_DK) * (A_DK ** -0.5)
    kc = heads(k, A_DK)
    lfc = heads(logf, A_DK)
    ic = heads(i, A_DV)
    causal = jnp.tril(jnp.ones((CHUNK, CHUNK), dtype=bool))

    def step(state, inp):
        qt, kt, lft, it = inp
        b = jnp.cumsum(lft, axis=-2)
        o_inter = jnp.einsum('bhtk,bhkv->bhtv', qt * jnp.exp(b), state)
        diff = b[..., :, None, :] - b[..., None, :, :]
        dec = jnp.exp(jnp.where(causal[:, :, None], diff, -jnp.inf))
        attn = jnp.einsum('bhtk,bhsk,bhtsk->bhts', qt, kt, dec)
        o = o_inter + jnp.einsum('bhts,bhsv->bhtv', attn, it)
        b_last = b[..., -1:, :]
        new_state = (jnp.exp(b_last[..., 0, :])[..., None] * state
                     + jnp.einsum('bhsk,bhsv->bhkv', kt * jnp.exp(b_last - b), it))
        return new_state, o

    s0 = jnp.zeros((bsz, A_HEADS, A_DK, A_DV), f32)
    _, o = lax.scan(step, s0, (qc, kc, lfc, ic))
    o = o.transpose(1, 0, 3, 2, 4).reshape(bsz, seq, A_HEADS, A_DV)
    o = head_rms(o, onorm_g).reshape(bsz, seq, A_WIDTH) * jax.nn.silu(g.astype(f32))
    return o.astype(q.dtype)

def band_attention(q, k, v, qn_g, kn_g, rel_bias):
    f32 = jnp.float32
    bsz, seq, _ = q.shape
    nc = seq // CHUNK
    qh = head_rms(q.reshape(bsz, seq, B_HEADS, B_HD), qn_g)
    kh = head_rms(k.reshape(bsz, seq, B_HEADS, B_HD), kn_g)
    vh = v.reshape(bsz, seq, B_HEADS, B_HD).astype(f32)
    pad = B_LEFT_CHUNKS * CHUNK
    kp = jnp.pad(kh, ((0, 0), (pad, 0), (0, 0), (0, 0)))
    vp = jnp.pad(vh, ((0, 0), (pad, 0), (0, 0), (0, 0)))
    band_idx = (jnp.arange(nc) * CHUNK)[:, None] + jnp.arange(B_BAND)[None, :]
    kb = kp[:, band_idx]
    vb = vp[:, band_idx]
    qc = qh.reshape(bsz, nc, CHUNK, B_HEADS, B_HD)
    scores = jnp.einsum('bnqhd,bnkhd->bnhqk', qc, kb) * (B_HD ** -0.5)
    rel = (pad + jnp.arange(CHUNK))[:, None] - jnp.arange(B_BAND)[None, :]
    bias = rel_bias.astype(f32)[:, jnp.clip(rel, -MAX_REL, MAX_REL) + MAX_REL]
    valid = band_idx >= pad
    scores = jnp.where(valid[None, :, None, None, :], scores + bias[None, None], -1e30)
    probs = jax.nn.softmax(scores, axis=-1)
    o = jnp.einsum('bnhqk,bnkhd->bnqhd', probs, vb)
    return o.reshape(bsz, seq, B_WIDTH).astype(q.dtype)

def second_inputs(seed: int = 0) -> dict:
    key = jax.random.key(seed)
    ks = jax.random.split(key, 24)
    f32 = jnp.float32

    def nrm(k, shape, scale):
        return jax.random.normal(k, shape, f32) * scale

    def gain(k, shape):
        return 1.0 + 0.02 * jax.random.normal(k, shape, f32)

    return {
        "x": nrm(ks[0], (BATCH, SEQ, D_MODEL), 1.0),
        "p": nrm(ks[1], (DEPTH_2, BATCH, SEQ, PLE_DIM), 1.0),
        "norm_mix_g": gain(ks[2], (DEPTH_2, D_MODEL)),
        "w_in": nrm(ks[3], (DEPTH_2, D_MODEL, D_IN), D_MODEL ** -0.5),
        "hgrn_lb_logits": nrm(ks[4], (DEPTH_2, A_HEADS * A_DK), 0.5),
        "hgrn_onorm_g": gain(ks[5], (DEPTH_2, A_DV)),
        "attn_qnorm_g": gain(ks[6], (DEPTH_2, B_HD)),
        "attn_knorm_g": gain(ks[7], (DEPTH_2, B_HD)),
        "attn_rel_bias": nrm(ks[8], (DEPTH_2, B_HEADS, N_REL), 0.3),
        "w_branch_a": nrm(ks[9], (DEPTH_2, A_WIDTH, D_MODEL), A_WIDTH ** -0.5),
        "w_branch_b": nrm(ks[10], (DEPTH_2, B_WIDTH, D_MODEL), B_WIDTH ** -0.5),
        "w_out": nrm(ks[11], (DEPTH_2, D_MODEL, D_MODEL), 0.5 * D_MODEL ** -0.5),
        "norm_ffn_g": gain(ks[12], (DEPTH_2, D_MODEL)),
        "w_ffn_gate": nrm(ks[13], (DEPTH_2, D_MODEL, D_FF), D_MODEL ** -0.5),
        "w_ffn_up": nrm(ks[14], (DEPTH_2, D_MODEL, D_FF), D_MODEL ** -0.5),
        "w_ffn_down": nrm(ks[15], (DEPTH_2, D_FF, D_MODEL), 0.5 * D_FF ** -0.5),
        "norm_ple_g": gain(ks[16], (DEPTH_2, D_MODEL)),
        "w_ple_gate": nrm(ks[17], (DEPTH_2, D_MODEL, D_MODEL), D_MODEL ** -0.5),
        "w_ple_proj": nrm(ks[18], (DEPTH_2, PLE_DIM, D_MODEL), 0.5 * PLE_DIM ** -0.5),
    }

def second_block(x, p, norm_mix_g, w_in, hgrn_lb_logits, hgrn_onorm_g, attn_qnorm_g, attn_knorm_g,
              attn_rel_bias, w_branch_a, w_branch_b, w_out, norm_ffn_g, w_ffn_gate, w_ffn_up,
              w_ffn_down, norm_ple_g, w_ple_gate, w_ple_proj):
    lb_soft = jax.nn.softmax(hgrn_lb_logits.astype(jnp.float32), axis=0)
    lb_cum = jnp.cumsum(lb_soft, axis=0)
    lower_bounds = lb_cum - lb_cum[0:1]
    split_at = [int(s) for s in np.cumsum(IN_SIZES)[:-1]]

    for li in range(DEPTH_2):
        h = rmsnorm(x, norm_mix_g[li])
        z = h @ w_in[li]
        qa, fa, ia, ga, qb, kb, vb, gate_a, gate_b = jnp.split(z, split_at, axis=-1)
        oa = hgrn2_mixer(qa, fa, ia, ga, lower_bounds[li], hgrn_onorm_g[li])
        ob = band_attention(qb, kb, vb, attn_qnorm_g[li], attn_knorm_g[li], attn_rel_bias[li])
        merged = (jax.nn.sigmoid(gate_a) * (oa @ w_branch_a[li])
                  + jax.nn.sigmoid(gate_b) * (ob @ w_branch_b[li]))
        x = x + merged @ w_out[li]
        h2 = rmsnorm(x, norm_ffn_g[li])
        x = x + (jax.nn.silu(h2 @ w_ffn_gate[li]) * (h2 @ w_ffn_up[li])) @ w_ffn_down[li]
        h3 = rmsnorm(x, norm_ple_g[li])
        x = x + jax.nn.sigmoid(h3 @ w_ple_gate[li]) * (p[li].astype(x.dtype) @ w_ple_proj[li])
    return x


def setup_inputs(seed=0):
    out = dict(first_inputs(seed))
    for name, value in second_inputs(seed + 1).items():
        if name != "x":
            out[name + "_2"] = value
    return out


def reference(
    x, c, ada_w, ada_b, norm_g, m_in_w, m_conv_w, m_conv_b, m_dt_bias, m_a_log, m_d, m_norm_g,
    m_out_w, kv_ada_w, kv_ada_b, kv_norm_g, kv_w, sb_in_w, sb_out_w, final_g, p_2, norm_mix_g_2,
    w_in_2, hgrn_lb_logits_2, hgrn_onorm_g_2, attn_qnorm_g_2, attn_knorm_g_2, attn_rel_bias_2,
    w_branch_a_2, w_branch_b_2, w_out_2, norm_ffn_g_2, w_ffn_gate_2, w_ffn_up_2, w_ffn_down_2,
    norm_ple_g_2, w_ple_gate_2, w_ple_proj_2,
):
    x = first_block(
        x, c, ada_w, ada_b, norm_g, m_in_w, m_conv_w, m_conv_b, m_dt_bias, m_a_log, m_d,
        m_norm_g, m_out_w, kv_ada_w, kv_ada_b, kv_norm_g, kv_w, sb_in_w, sb_out_w, final_g,
    )
    return second_block(
        x, p_2, norm_mix_g_2, w_in_2, hgrn_lb_logits_2, hgrn_onorm_g_2, attn_qnorm_g_2,
        attn_knorm_g_2, attn_rel_bias_2, w_branch_a_2, w_branch_b_2, w_out_2, norm_ffn_g_2,
        w_ffn_gate_2, w_ffn_up_2, w_ffn_down_2, norm_ple_g_2, w_ple_gate_2, w_ple_proj_2,
    )


_drawn_inputs = setup_inputs


def setup_inputs(seed=0):
    import zlib

    import numpy as np

    out = dict(_drawn_inputs(seed))
    spreads = {}
    factors = {'ada_b': 4.221,
     'm_conv_b': 8.0,
     'm_d': 2.723,
     'm_norm_g': 3.727,
     'kv_ada_b': 8.0,
     'kv_norm_g': 7.299,
     'norm_mix_g_2': 7.525,
     'hgrn_onorm_g_2': 8.0,
     'attn_qnorm_g_2': 8.0,
     'attn_knorm_g_2': 8.0,
     'attn_rel_bias_2': 6.792,
     'norm_ffn_g_2': 7.11,
     'norm_ple_g_2': 64.0,
     'p_2': 3.873,
     'w_ple_gate_2': 5.779,
     'w_ple_proj_2': 3.864}
    for name, (base, spread) in spreads.items():
        noise = np.random.default_rng([zlib.crc32(name.encode()), seed]).standard_normal(out[name].shape)
        drawn = base * np.exp(spread * noise) if base else spread * noise
        out[name] = __import__('jax').numpy.asarray(drawn.astype(out[name].dtype))
    for name, factor in factors.items():
        out[name] = (out[name] * factor).astype(out[name].dtype)
    return out
```

```python
from contextlib import ExitStack

import numpy as np

import concourse.bass as bass
from concourse import mybir

F32 = mybir.dt.float32
F32R = mybir.dt.float32r
U8 = mybir.dt.uint8
ALU = mybir.AluOpType
ACT = mybir.ActivationFunctionType
AX = mybir.AxisListType.X

S = 512
D = 1024
EPS = 1e-6
DFF = 2816
NB = D // 128


def _cols(name, c0, n, k0=0, kb=8):
    return (name, k0, kb, ((c0, n),))


def weight_plan():
    plan = [("dt", ("m_in_w", 0, 8, ((5120, 32), (0, 96))))]
    for g in range(4):
        plan.append(("bc", ("m_in_w", 0, 8, ((4096 + 128 * g, 128), (4608 + 128 * g, 128)))))
        for i in range(2):
            plan.append(("xs", _cols("m_in_w", 2048 + 512 * g + 256 * i, 256)))
        for i in range(2):
            plan.append(("z", _cols("m_in_w", 512 * g + 256 * i, 256)))
    for g in range(4):
        for i in range(2):
            plan.append(("out", _cols("m_out_w", 512 * i, 512, 4 * g, 4)))
    for i in range(8):
        plan.append(("kv", _cols("kv_w", 256 * i, 256)))
    for i in range(4):
        plan.append(("q", _cols("sb_in_w", 256 * i, 256)))
    for i in range(4):
        plan.append(("sz", _cols("sb_in_w", 1024 + 256 * i, 256)))
    for i in range(4):
        plan.append(("so", _cols("sb_out_w", 256 * i, 256)))
    for i in range(18):
        plan.append(("in2", _cols("w_in_2", 256 * i, 256)))
    for i in range(2):
        plan.append(("wa", _cols("w_branch_a_2", 512 * i, 512, 0, 4)))
    for i in range(2):
        plan.append(("in2", _cols("w_in_2", 4608 + 512 * i, 256)))
        plan.append(("in2", _cols("w_in_2", 4864 + 512 * i, 256)))
        plan.append(("wb", _cols("w_branch_b_2", 512 * i, 512, 0, 4)))
    for i in range(4):
        plan.append(("wo2", _cols("w_out_2", 256 * i, 256)))
    for i in range(11):
        plan.append(("fg", _cols("w_ffn_gate_2", 256 * i, 256)))
        plan.append(("fu", _cols("w_ffn_up_2", 256 * i, 256)))
    for i in range(4):
        for k0, kb in ((0, 8), (8, 8), (16, 6)):
            plan.append(("fd", _cols("w_ffn_down_2", 256 * i, 256, k0, kb)))
    plan.append(("pp", _cols("w_ple_proj_2", 0, 1024, 0, 2)))
    for i in range(4):
        plan.append(("pg", _cols("w_ple_gate_2", 256 * i, 256)))
    return plan


def chunk_words(spec):
    return spec[2] * sum(n for _, n in spec[3])


VEC = [("c", 8), ("ada_b", 48), ("norm_g", 16), ("conv_w", 96), ("conv_b", 24), ("m_d", 16),
       ("m_norm_g", 16), ("kv_ada_b", 16), ("kv_norm_g", 8), ("final_g", 8), ("mix_g", 8),
       ("lb", 4), ("onorm", 1), ("qn", 1), ("kn", 1), ("ffn_g", 8), ("ple_g", 8), ("dtb", 1), ("alog", 1)]
CON = [("ident", 128), ("ones", 128), ("bones", 128), ("cmask", 128), ("smask", 512), ("amask", 128)]


def offsets(table):
    out, at = {}, 0
    for name, n in table:
        out[name] = (at, n)
        at += n
    return out, at


VOFF, VLEN = offsets(VEC)
COFF, CLEN = offsets(CON)


class Later(list):
    pass


class Queue:

    def __init__(self, name, sem):
        self.name, self.sem, self.n, self.items, self.seen = name, sem, 0, [], {}
        self.held = []

    def wait(self, *after):
        for t in after:
            if t is None:
                continue
            if isinstance(t, Later) and not t:
                self.holder.flush()
                assert t
            if isinstance(t, list):
                self.wait(*t)
                continue
            sem, value = t
            if self.seen.get(id(sem), 0) < value:
                self.seen[id(sem)] = value
                self.items.append((None, sem, value))

    def do(self, fn, *after):
        self.wait(*after)
        self.n += 1
        self.items.append((fn, self.sem, 1))
        return (self.sem, self.n)

    def many(self, fns, *after):
        self.wait(*after)
        for fn in fns[:-1]:
            self.items.append((fn, None, 0))
        self.n += 1
        self.items.append((fns[-1], self.sem, 1))
        return (self.sem, self.n)

    def quiet(self, fn, *after):
        self.wait(*after)
        self.items.append((fn, None, 0))

    def later(self, fn, *after):
        mark = Later()
        self.flush()
        self.held.append((mark, fn, after))
        return mark

    def flush(self):
        while self.held:
            mark, fn, after = self.held.pop(0)
            mark.append(self.do(fn, *after))

    def last(self):
        self.flush()
        return (self.sem, self.n) if self.n else None

    def dma(self, fn, sem, count, *after):
        self.wait(*after)
        self.items.append((fn, sem, 16))
        return (sem, 16 * count)

    def play(self, eng):
        for fn, sem, value in self.items:
            if fn is None:
                eng.wait_ge(sem, value)
            else:
                i = fn(eng)
                if sem is not None:
                    i.then_inc(sem, value)


class Slot:

    def __init__(self, ap):
        self.ap, self.rel = ap, []

    def take(self):
        r, self.rel = self.rel, []
        return r


class Ring:
    def __init__(self, slots):
        self.slots, self.i = slots, -1

    def next(self):
        self.i += 1
        return self.slots[self.i % len(self.slots)]


def program(nc, wstream, astream, vec, con, masks, xT, pT, rbx, out, scratch, pscr):
    ctx = ExitStack()
    with ctx:
        sbt = lambda n, shape, dt=F32, c=ctx: c.enter_context(nc.sbuf_tensor(n, shape, dt))
        sem = lambda n: ctx.enter_context(nc.semaphore(n))
        PE, V, A, G, SP = (Queue(n, sem("s_" + n)) for n in ("pe", "dve", "act", "pool", "sp"))
        for q in (PE, V, A, G, SP):
            q.holder = V

        RAW = 2
        raw = sbt("raw", [128, RAW, 2048])
        whi = sbt("whi", [128, 2, 2048], F32R)
        wlo = sbt("wlo", [128, 2, 2048], F32R)
        X = sbt("X", [128, NB, S])
        HH = sbt("HH", [128, NB, S], F32R)
        HL = sbt("HL", [128, NB, S], F32R)
        cv = sbt("cv", [128, VLEN])
        cc = sbt("cc", [128, CLEN])
        mk = sbt("mk", [128, 7, 128], U8)
        ada = sbt("ada", [128, 64])
        G1 = sbt("G1", [128, 32])
        cact = sbt("cact", [128, 8])
        SQ = sbt("SQ", [128, S])
        R = sbt("R", [128, S])
        tmpr = Ring([Slot(sbt(f"tmp{i}", [128, S])) for i in range(3)])
        banks = [ctx.enter_context(nc.psum_tensor(f"bank{i}", [128, S], F32)) for i in range(8)]
        dense = Ring([Slot(b) for b in banks[:3]])
        aux = [Slot(b) for b in banks[3:]]

        vcol = lambda name: cv[:, VOFF[name][0]:VOFF[name][0] + VOFF[name][1]]
        ccol = lambda name: cc[:, COFF[name][0]:COFF[name][0] + COFF[name][1]]
        ident, ones, bones = ccol("ident"), ccol("ones"), ccol("bones")
        cmask, smask, amask = ccol("cmask"), ccol("smask"), ccol("amask")

        ld = []
        m0, m1 = tmpr.slots[0], tmpr.slots[1]
        for n, (dst, src) in enumerate(((cv[:, :], vec), (cc[:, :], con), (m0.ap[:, :], masks[:, 0:512]),
                                        (m1.ap[:, 0:384], masks[:, 512:896]))):
            ld.append(A.dma(lambda e, d=dst, s=src: e.dma_start(d, s), sem(f"s_ld{n}"), 1))
        t_x = SP.dma(lambda e: e.dma_start(X[:, :, :], xT), sem("s_ldx"), 1)
        t_vec, t_con = ld[0:2]
        m0.rel = [V.do(lambda e: e.tensor_copy(mk[:, 0:4, :], m0.ap[:, :].rearrange("p (a b) -> p a b", a=4)), ld[2])]
        m1.rel = [V.do(lambda e: e.tensor_copy(mk[:, 4:7, :], m1.ap[:, 0:384].rearrange("p (a b) -> p a b", a=3)), ld[3])]
        t_mk = m1.rel[0]

        plan = weight_plan()
        starts, at = [], 0
        for _, spec in plan:
            starts.append(at)
            at += 128 * chunk_words(spec)
        s_raw = [sem(f"s_raw{i}") for i in range(RAW)]
        raw_rel = [[] for _ in range(RAW)]
        w_rel = [[], []]
        st = {"dma": 0, "split": 0, "use": 0, "pair": 0}
        loaded, split = {}, {}

        def emit_dma(upto):
            while st["dma"] <= min(upto, len(plan) - 1):
                i = st["dma"]
                n = chunk_words(plan[i][1])
                r = i % RAW
                src = wstream[starts[i]:starts[i] + 128 * n].rearrange("(p n) -> p n", p=128)
                loaded[i] = SP.dma(lambda e, r=r, n=n, src=src: e.dma_start(raw[:, r, 0:n], src),
                                   s_raw[r], i // RAW + 1, raw_rel[r])
                raw_rel[r] = []
                st["dma"] += 1

        def emit_split(upto):
            while st["split"] <= min(upto, len(plan) - 1):
                i = st["split"]
                st["split"] += 1
                emit_dma(i)
                n, r, b = chunk_words(plan[i][1]), i % RAW, st["pair"] % 2
                st["pair"] += 1
                free = w_rel[b]
                w_rel[b] = []
                th = A.do(lambda e, r=r, b=b, n=n: e.activation(whi[:, b, 0:n], raw[:, r, 0:n], ACT.Copy),
                          loaded[i], free)
                tl = G.do(lambda e, r=r, b=b, n=n: e.tensor_tensor(
                    wlo[:, b, 0:n], raw[:, r, 0:n], whi[:, b, 0:n].bitcast(F32), ALU.subtract),
                    loaded[i], th, free)
                raw_rel[r] = [th, tl]
                split[i] = (b, th, tl)

        def use(kind):
            i = st["use"]
            assert plan[i][0] == kind, (plan[i], kind)
            st["use"] += 1
            emit_split(i)
            emit_split(i + 1)
            emit_dma(i + 1)
            return i

        def next_bias(i):
            if i < 8:
                i = i // 2 + (0 if i % 2 else 4)
            if i < 12:
                o = VOFF["ada_b"][0] + 2 * i
            elif i < 20:
                o = VOFF["kv_ada_b"][0] + 2 * (i - 12)
            else:
                o = VOFF["ada_b"][0] + 24 + 2 * (i - 20)
            return 2 * i, cv[:, o:o + 2]

        ada_at = {"use": 0, "load": 0}
        ada_ready = {}

        def ada_load(slot, s, count, *after):
            i = ada_at["load"]
            ada_at["load"] += 1
            ada_ready[i] = (slot, SP.dma(lambda e: e.dma_start(slot.ap, astream[i]), s, count, slot.take(), *after))

        def ada_piece(then=None, bank=None):
            i = ada_at["use"]
            ada_at["use"] += 1
            slot, loaded = ada_ready.pop(i)
            col, bias = next_bias(i)
            w = slot.ap
            t = V.do(lambda e: e.tensor_scalar(w[:, 0:256], w[:, 0:256], cact[:, 0:1], None, ALU.mult), loaded, t_c)
            for k in range(1, 8):
                t = V.do(lambda e, k=k: e.scalar_tensor_tensor(
                    w[:, 0:256], w[:, 256 * k:256 * k + 256], cact[:, k:k + 1], w[:, 0:256], ALU.mult, ALU.add), t)
                if k % 2:
                    yield
            yield
            bank = bank or dense.next()
            tm = PE.many([lambda e, j=j, bank=bank: e.matmul(
                bank.ap[:, j:j + 1], w[:, 128 * j:128 * j + 128], ones[:, 0:1], start=True, stop=True)
                for j in range(2)], t, t_con, bank.take())
            slot.rel = [tm]
            yield
            bank.rel = [V.do(lambda e, bank=bank: e.tensor_tensor(ada[:, col:col + 2], bank.ap[:, 0:2], bias, ALU.add), tm, t_vec)]
            if then:
                then()
            yield

        def mm3(i, kb0, n0, n1, ncols, h, bank_ap, t0, t1, kfirst, klast, token_major):
            b = split[i][0]
            hh, hl = h
            kb = plan[i][1][2]
            wh = whi[:, b, 0:kb * ncols].rearrange("p (k n) -> p k n", k=kb)
            wl = wlo[:, b, 0:kb * ncols].rearrange("p (k n) -> p k n", k=kb)
            fns = []
            for k in range(kb):
                for m, (w, x) in enumerate(((wh, hh), (wh, hl), (wl, hh))):
                    wa, xa = w[:, k, n0:n1], x[:, kb0 + k, t0:t1]
                    l, r = (xa, wa) if token_major else (wa, xa)
                    fns.append(lambda e, l=l, r=r, o=bank_ap, s=(kfirst and k == 0 and m == 0),
                               z=(klast and k == kb - 1 and m == 2): e.matmul(o, l, r, start=s, stop=z))
            return fns

        def chain(*gens):
            for g in gens:
                yield from g

        def run(gen):
            try:
                while True:
                    next(gen)
            except StopIteration as stop:
                return stop.value

        def gblocks(i, js, ncols, h, ht, bks, first=True, last=True, kb0=0):
            PE.wait(split[i][1], split[i][2], *[b.take() for b in bks] if first else [])
            fns = [mm3(i, kb0, 128 * j, 128 * j + 128, ncols, h, b.ap[:, :], 0, S, first, last, False)
                   for j, b in zip(js, bks)]
            kb = plan[i][1][2]
            for k in range(kb):
                PE.wait(ht[kb0 + k])
                for n in range(len(js)):
                    for m in range(3):
                        if (k, n, m) == (kb - 1, len(js) - 1, 2):
                            t = PE.do(fns[n][3 * k + m])
                        else:
                            PE.quiet(fns[n][3 * k + m])
                if k < kb - 1:
                    yield
            w_rel[split[i][0]] = [t]
            return t

        def gblock(i, j, ncols, h, ht, bank, first=True, last=True, kb0=0):
            return (yield from gblocks(i, (j,), ncols, h, ht, (bank,), first, last, kb0))

        def blocks(*args, **more):
            return run(gblocks(*args, **more))

        def block(*args, **more):
            return run(gblock(*args, **more))

        def block_tok(i, tb, ncols, h, ht, bank, half, first):
            fns = mm3(i, 0, 0, ncols, ncols, h, bank.ap[:, 256 * half:256 * half + ncols],
                      128 * tb, 128 * tb + 128, True, True, True)
            t = PE.many(fns, split[i][1], split[i][2], ht, bank.take() if first else None)
            w_rel[split[i][0]] = [t]
            return t

        class SumSq:

            def __init__(self, n, acc=None, onesm=None):
                self.n, self.k, self.onesm = n, 0, ones if onesm is None else onesm
                self.acc, self.t, self.free = SQ if acc is None else acc, None, None

            def add(self, src, after, scale=None):
                k, self.k = self.k, self.k + 1
                sc = 1.0 if scale is None else scale
                if k == 0 and self.n > 1:
                    self.t = A.do(lambda e: e.activation(self.acc[:, :], src, ACT.Square, scale=sc), after, PE.last())
                    return
                q = tmpr.next()
                t = A.do(lambda e: e.activation(q.ap[:, :], src, ACT.Square, scale=sc), after, q.take())
                if k < self.n - 1:
                    self.t = G.do(lambda e: e.tensor_tensor(self.acc[:, :], self.acc[:, :], q.ap[:, :], ALU.add), t, self.t)
                    q.rel = [self.t]
                else:
                    self.q, self.tq = q, t

            def sum(self, bank):
                assert self.k == self.n
                free = bank.take()
                if self.n > 1:
                    PE.do(lambda e: e.matmul(bank.ap[:, :], self.onesm, self.acc[:, :], start=True, stop=False),
                          self.t, t_con, free)
                t = PE.do(lambda e: e.matmul(bank.ap[:, :], self.onesm, self.q.ap[:, :], start=(self.n == 1), stop=True),
                          self.tq, t_con, free)
                self.q.rel = [t]
                return t

        def rsqrt(bank, count, dst, after, free):
            t = A.do(lambda e: e.activation(dst, bank.ap[:, :], ACT.Ln, scale=1.0 / count, bias=eps_ap), after,
                     t_eps, free)
            bank.rel = [t]
            return A.do(lambda e: e.activation(dst, dst, ACT.Exp, scale=-0.5), t)

        lnexp = lambda: A.items.append((lambda e: e.preload_act_table_set("natural_log_exp_and_others"), None, 0))
        exptanh = lambda: A.items.append((lambda e: e.preload_act_table_set("exp_and_others"), None, 0))

        def modulated(gains, shift, hfree, xt, rt, ks=range(NB)):
            out_t = []
            for k in ks:
                q = tmpr.next()
                t = V.do(lambda e, q=q, k=k: e.scalar_tensor_tensor(
                    q.ap[:, :], X[:, k, :], gains[:, k:k + 1], R[:, :], ALU.mult, ALU.mult), xt, rt, q.take())
                if shift is None:
                    th = A.do(lambda e, q=q, k=k: e.activation(HH[:, k, :], q.ap[:, :], ACT.Copy), t, hfree)
                    tl = (G.do if k % 2 else V.later)(lambda e, q=q, k=k: e.tensor_tensor(
                        HL[:, k, :], q.ap[:, :], HH[:, k, :].bitcast(F32), ALU.subtract), t, th, hfree)
                else:
                    th = A.do(lambda e, q=q, k=k: e.activation(
                        HH[:, k, :], q.ap[:, :], ACT.Identity, bias=shift[:, k:k + 1]), t, hfree)
                    tl = V.later(lambda e, q=q, k=k: e.scalar_tensor_tensor(
                        HL[:, k, :], q.ap[:, :], shift[:, k:k + 1], HH[:, k, :].bitcast(F32),
                        ALU.add, ALU.subtract), t, th, hfree)
                q.rel = [th, tl]
                out_t.append([th, tl])
            return out_t

        def fence(*queues):
            marks = [q.last() for q in (PE, V, A, G)]
            for q in queues or (V, A, G):
                q.wait(*[m for m in marks if m])
            return marks

        def gain(dst, g, scale, t):
            return V.do(lambda e: e.scalar_tensor_tensor(dst, scale, 1.0, g, ALU.add, ALU.mult), t, t_vec)

        eps = sbt("eps", [128, 1])
        eps_ap = eps[:, 0:1]
        t_eps = V.do(lambda e: e.memset(eps[:, :], EPS))
        sg = sbt("sg", [128, 8])
        t = A.do(lambda e: e.activation(sg[:, :], vcol("c"), ACT.Sigmoid), t_vec)
        t_c = V.do(lambda e: e.tensor_tensor(cact[:, :], sg[:, :], vcol("c"), ALU.mult), t, t_vec)
        lnexp()
        ph = ExitStack()
        psb = lambda n, shape, dt=F32: sbt(n, shape, dt, ph)
        for n in range(8):
            ada_load(Slot(psb(f"A{n}", [128, 2048])[:, :]), sem(f"s_a{n}"), 1)
        ss = SumSq(NB)
        for k in range(NB):
            ss.add(X[:, k, :], t_x)
        t = ss.sum(aux[0])
        rt = rsqrt(aux[0], D, R[:, :], t, None)

        def ada_first(i, bank):
            slot, loaded = ada_ready.pop(i)
            ada_at["use"] += 1
            col, bias = next_bias(i)
            w = slot.ap
            fns = [lambda e, j=j, k=k: e.matmul(
                bank.ap[:, j:j + 1], w[:, 256 * k + 128 * j:256 * k + 128 * j + 128], cact[:, k:k + 1],
                start=(k == 6), stop=False) for j in range(2) for k in (6, 7)]
            last = [lambda e, j=j: e.matmul(
                bank.ap[:, j:j + 1], w[:, 128 * j:128 * j + 128], ones[:, 0:1], start=False, stop=True) for j in range(2)]
            t = V.do(lambda e: e.tensor_scalar(w[:, 0:256], w[:, 0:256], cact[:, 0:1], None, ALU.mult), loaded, t_c)
            for k in range(1, 6):
                t = V.do(lambda e, k=k: e.scalar_tensor_tensor(
                    w[:, 0:256], w[:, 256 * k:256 * k + 256], cact[:, k:k + 1], w[:, 0:256], ALU.mult, ALU.add), t)
            PE.wait(loaded, t_c, t_con, bank.take())
            for j in range(2):
                PE.quiet(fns[2 * j])
                PE.quiet(fns[2 * j + 1])
                tm = PE.do(last[j], t)
            return bank, tm, col, bias

        def finish_first(i, parts):
            for bank, tm, col, bias in parts:
                t = V.do(lambda e, bias=bias, bank=bank, col=col: e.tensor_tensor(ada[:, col:col + 2], bank.ap[:, 0:2], bias, ALU.add), tm, t_vec)
                bank.rel = [t]
            o = VOFF["norm_g"][0] + 2 * i
            V.wait(gain(G1[:, 2 * i:2 * i + 2], cv[:, o:o + 2], ada[:, 8 + 2 * i:10 + 2 * i], t))
            return modulated(G1[:, 0:8], ada[:, 0:8], None, t_x, rt, range(2 * i, 2 * i + 2))

        ht, parts = [], []
        for i in range(4):
            parts.append([ada_first(2 * i + n, aux[1 + (2 * i + n) % 4]) for n in range(2)])
            if i > 0:
                ht += finish_first(i - 1, parts[i - 1])
        ht += finish_first(3, parts[3])
        t_fence = fence()
        ph.close()

        ph = ExitStack()
        psb = lambda n, shape, dt=F32: sbt(n, shape, dt, ph)
        Y = psb("Y", [128, 16, S])
        XS = [psb(f"XS{i}", [128, 4, S]) for i in range(2)]
        BC = [psb(f"BC{i}", [128, 2, S]) for i in range(2)]
        AC = [psb(f"AC{i}", [128, 8, 128]) for i in range(2)]
        aslot = Slot(psb("aslot", [128, 2048])[:, :])
        s_as = sem("s_as")
        as_n = [0]

        def ada_next(*after):
            if ada_at["load"] == 20:
                return
            as_n[0] += 1
            ada_load(aslot, s_as, as_n[0], *after)

        ada_next(t_fence)
        E = psb("E", [128, 8, 128])
        EA = psb("EA", [128, 4, 128])
        XD = [psb(f"XD{i}", [128, 8, 64]) for i in range(2)]
        XW = psb("XW", [128, 8, 64])
        BT = psb("BT", [128, 128])
        CB = psb("CB", [128, 128])
        YT = psb("YT", [128, 4, 128])
        ST = psb("ST", [128, 8, 64])
        U = [Slot(psb(f"U{i}", [128, S + 3])) for i in range(2)]
        cbh = psb("cbh", [128, 24])
        WE = psb("WE", [128, 4, 8])
        EL = psb("EL", [128, 4, 8])
        dtk = psb("dtk", [128, 4, 32])
        atk = psb("atk", [128, 4, 32])

        i = use("dt")
        bank = dense.next()
        t = block(i, 0, 128, (HH, HL), ht, bank)
        xb, dd, ac = (YT[0:32, :, :].rearrange("p a b -> p (a b)"), EA[0:32, :, :].rearrange("p a b -> p (a b)"),
                      E[0:32, 0:4, :].rearrange("p a b -> p (a b)"))
        dtb, alog = cv[0:32, VOFF["dtb"][0]:VOFF["dtb"][0] + 1], cv[0:32, VOFF["alog"][0]:VOFF["alog"][0] + 1]
        tb_ = V.do(lambda e, bank=bank: e.tensor_scalar(xb, bank.ap[0:32, :], dtb, None, ALU.add), t)
        bank.rel = [tb_]
        t = A.do(lambda e: e.activation(dd, xb, ACT.Abs), tb_)
        t = A.do(lambda e: e.activation(dd, dd, ACT.Exp, scale=-1.0), t)
        t = A.do(lambda e: e.activation(dd, dd, ACT.Ln, bias=1.0), t)
        t_dt = V.do(lambda e: e.scalar_tensor_tensor(dd, xb, 0.0, dd, ALU.max, ALU.add), t)
        aneg = cbh[0:32, 0:1]
        t = A.do(lambda e: e.activation(sg[0:32, 0:1], alog, ACT.Exp), t_c)
        t = V.do(lambda e: e.tensor_scalar(xb, dd, sg[0:32, 0:1], -1.0, ALU.mult, ALU.mult), t, t_dt)
        for c in range(4):
            t_ac = V.do(lambda e, c=c: e.tensor_tensor_scan(
                ac[:, 128 * c:128 * c + 128], smask[0:32, 0:128], xb[:, 128 * c:128 * c + 128], 0.0,
                ALU.mult, ALU.add), t, t_con)
        s_sc = sem("s_sc")
        t_sc = SP.dma(lambda e: e.dma_start(scratch, ac), s_sc, 1, t_ac)
        bank = dense.next()
        fns = []
        for n, src in ((0, dd), (1, ac)):
            for c in range(4):
                o = 128 * n + 32 * c
                fns.append(lambda e, o=o, src=src, c=c, b=bank: e.transpose(
                    b.ap[:, o:o + 32], src[:, 128 * c:128 * c + 128], ident[0:32, 0:32]))
        t = PE.many(fns, t_ac, t_dt, t_con, bank.take())
        t1 = V.do(lambda e, b=bank: e.tensor_copy(dtk[:, :, :], b.ap[:, 0:128].rearrange("p (c h) -> p c h", c=4)), t)
        t_tk = V.do(lambda e, b=bank: e.tensor_copy(atk[:, :, :], b.ap[:, 128:256].rearrange("p (c h) -> p c h", c=4)), t)
        bank.rel = [t1, t_tk]
        for u in U:
            t_u = V.do(lambda e, u=u: e.memset(u.ap[:, 0:3], 0.0))
            u.rel = [t_u]
        t_cbh = V.do(lambda e: e.tensor_scalar(cbh[:, :], vcol("conv_b"), 0.5, None, ALU.mult), t_vec)
        exptanh()

        def conv_silu(bank, t, blk, dst, free):
            u = next_u()
            tu = A.do(lambda e: e.activation(u.ap[:, 3:S + 3], bank.ap[:, :], ACT.Copy, scale=0.5), t, u.take())
            bank.rel = [tu]
            q = tmpr.next()
            w = lambda j: cv[:, VOFF["conv_w"][0] + 24 * j + blk:VOFF["conv_w"][0] + 24 * j + blk + 1]
            t = V.do(lambda e: e.tensor_scalar(q.ap[:, :], u.ap[:, 3:S + 3], w(3), cbh[:, blk:blk + 1],
                                               ALU.mult, ALU.add), tu, t_cbh, q.take())
            for j in (2, 1, 0):
                t = V.do(lambda e, j=j: e.scalar_tensor_tensor(q.ap[:, :], u.ap[:, j:j + S], w(j), q.ap[:, :],
                                                               ALU.mult, ALU.add), t)
            u.rel = [t]
            h = tmpr.next()
            ta = A.do(lambda e: e.activation(h.ap[:, :], q.ap[:, :], ACT.Tanh), t, h.take())
            t = V.later(lambda e: e.scalar_tensor_tensor(dst, h.ap[:, :], 1.0, q.ap[:, :], ALU.add, ALU.mult), ta, free)
            q.rel = [t]
            h.rel = [t]
            return t

        uring = Ring(U)
        next_u = uring.next

        def twice_silu(bank, t, dst, free):
            h = tmpr.next()
            ta = A.do(lambda e: e.activation(h.ap[:, :], bank.ap[:, :], ACT.Tanh, scale=0.5), t, h.take())
            t = V.later(lambda e: e.scalar_tensor_tensor(dst, h.ap[:, :], 1.0, bank.ap[:, :], ALU.add, ALU.mult), ta, free)
            bank.rel = [t]
            h.rel = [t]
            return t

        def twice_silu_into(q, bank, t):
            ta = A.do(lambda e: e.activation(q.ap[:, :], bank.ap[:, :], ACT.Tanh, scale=0.5), t, q.take())
            t = V.later(lambda e: e.scalar_tensor_tensor(q.ap[:, :], q.ap[:, :], 1.0, bank.ap[:, :], ALU.add, ALU.mult), ta)
            bank.rel = [t]
            return t

        H = (HH, HL)
        xs_t, bc_t, y_t = {}, {}, {}
        xs_rel, bc_rel = [[], []], [[], []]
        ssd_done = {}

        def in_proj(g):
            p = g % 2
            i = use("bc")
            fb = bc_rel[p]
            bc_t[g] = []
            for j in range(2):
                bank = dense.next()
                t = yield from gblock(i, j, 256, H, ht, bank)
                bc_t[g].append(conv_silu(bank, t, 16 + 4 * j + g, BC[p][:, j, :], fb))
                yield
            xs_t[g] = []
            for c in range(2):
                i = use("xs")
                for j in range(2):
                    n = 2 * c + j
                    bank = dense.next()
                    t = yield from gblock(i, j, 256, H, ht, bank)
                    xs_t[g].append(conv_silu(bank, t, 4 * g + n, XS[p][:, n, :], xs_rel[p]))
                    yield
            y_t[g] = []
            for c in range(2):
                i = use("z")
                for j in range(2):
                    bank = dense.next()
                    t = yield from gblock(i, j, 256, H, ht, bank)
                    y_t[g].append(twice_silu(bank, t, Y[:, 4 * g + 2 * c + j, :], None))
                    yield

        s_ac = [sem("s_ac0"), sem("s_ac1")]
        ac_rel = [[], []]
        e_rel = [None]
        prev = {}

        def ssd(g):
            p = g % 2
            xs, bc = XS[p], BC[p]

            def load(c):
                src = scratch[8 * g:8 * g + 8, 128 * c:128 * c + 128].partition_broadcast(128)
                b = c % 2
                t = SP.dma(lambda e: e.dma_start(AC[b][:, :, :], src), s_ac[b], 2 * g + c // 2 + 1, t_sc, ac_rel[b], t_ac)
                ac_rel[b] = []
                return t

            loads = {0: load(0), 1: load(1)}
            yield

            def prep(c):
                xd, AC_, t_bc = XD[c % 2], AC[c % 2], loads[c]
                cs = slice(128 * c, 128 * c + 128)
                lastc = AC_[:, :, 127]
                tw = tel = None
                if c < 3:
                    tw = V.do(lambda e: e.tensor_tensor(WE[:, c, :], lastc, atk[:, c, 8 * g:8 * g + 8], ALU.subtract),
                              t_bc, t_tk, prev.get("xw"))
                    tw = A.do(lambda e: e.activation(WE[:, c, :], WE[:, c, :], ACT.Exp), tw)
                    tel = A.do(lambda e: e.activation(EL[:, c, :], lastc, ACT.Exp), t_bc, prev.get("st"))
                bx, bb = aux[0], aux[1]
                tx = PE.many([lambda e, j=j: e.transpose(bx.ap[:, 128 * j:128 * j + 128], xs[:, j, cs], ident)
                              for j in range(4)], xs_t[g], bx.take(), t_con)
                fns = []
                if c < 3:
                    fns.append(lambda e: e.transpose(bb.ap[:, 0:128], bc[:, 0, cs], ident))
                fns.append(lambda e: e.matmul(bb.ap[:, 128:256], bc[:, 0, cs], bc[:, 1, cs], start=True, stop=True))
                tb = PE.many(fns, bc_t[g], bb.take())
                for h in range(8):
                    td = V.do(lambda e, h=h: e.tensor_scalar(
                        E[:, h, :], AC_[:, h, :], atk[:, c, 8 * g + h:8 * g + h + 1], 0.0, ALU.subtract, ALU.min),
                        t_bc, t_tk, prev.get("e"))
                te = A.do(lambda e: e.activation(E[:, :, :], E[:, :, :], ACT.Exp), td)
                tdx = V.do(lambda e: e.tensor_tensor(
                    xd[:, :, :], bx.ap[:, :].rearrange("p (h d) -> p h d", h=8),
                    dtk[:, c, 8 * g:8 * g + 8].unsqueeze(2).to_broadcast([128, 8, 64]), ALU.mult),
                    tx, t_tk, prev.get(("xd", c % 2)))
                bx.rel = [tdx]
                tcb = V.do(lambda e: e.tensor_tensor(CB[:, :], bb.ap[:, 128:256], cmask, ALU.mult),
                           tb, t_con, prev.get("cb"))
                bb.rel = [tcb]
                r = {"xd": tdx}
                if c < 3:
                    tbt = A.do(lambda e: e.activation(BT[:, :], bb.ap[:, 0:128], ACT.Copy), tb, tcb, prev.get("bt"))
                    bb.rel = [tcb, tbt]
                    txw = V.do(lambda e: e.tensor_tensor(
                        XW[:, :, :], xd[:, :, :], WE[:, c, :].unsqueeze(2).to_broadcast([128, 8, 64]), ALU.mult),
                        tdx, tw, prev.get("bt"))
                    r.update(bt=tbt, xw=txw)
                    prev["xw"] = txw
                if c > 0:
                    tea = A.do(lambda e: e.activation(EA[0:64, :, :], AC_[0:64, 0::2, :], ACT.Exp), t_bc, prev.get("ea"))
                    tea = A.do(lambda e: e.activation(EA[64:128, :, :], AC_[64:128, 1::2, :], ACT.Exp), tea)
                    r["ea"] = tea
                yield
                tm = V.do(lambda e: e.tensor_tensor(
                    E[:, :, :], E[:, :, :], CB[:, :].unsqueeze(1).to_broadcast([128, 8, 128]), ALU.mult), te, tcb)
                prev["cb"] = tm
                r["m"] = tm
                r["el"] = tel
                ac_rel[c % 2] = [td, te, tm, tel, tw] + ([tea] if c > 0 else [])
                return r

            def finish(c, r):
                xd = XD[c % 2]
                cs = slice(128 * c, 128 * c + 128)
                bd, bo, bs = aux[2], aux[3], aux[4]
                to = None
                if c < 3:
                    ts = PE.do(lambda e: e.matmul(bs.ap[:, :], BT[:, :], XW[:, :, :].rearrange("p a b -> p (a b)"),
                                                  start=True, stop=True), r["bt"], r["xw"], bs.take())
                    prev["bt"] = ts
                if c > 0:
                    to = PE.many([lambda e, q=q: e.matmul(
                        bo.ap[:, 128 * q:128 * q + 128], ST[:, 2 * q:2 * q + 2, :].rearrange("p a b -> p (a b)"),
                        bc[:, 1, cs], start=True, stop=True) for q in range(4)], prev["st"], bo.take())
                    bov = bo.ap[:, :].rearrange("p (q t) -> p q t", q=4)
                    tyo = V.do(lambda e: e.tensor_tensor(YT[:, :, :], bov, EA[:, :, :], ALU.mult), to, r["ea"])
                    bo.rel = [tyo]
                    prev["ea"] = tyo
                if c < 3:
                    bsv = bs.ap[:, :].rearrange("p (h d) -> p h d", h=8)
                    if c == 0:
                        t = V.do(lambda e: e.tensor_copy(ST[:, :, :], bsv), ts, prev.get("sto"))
                    else:
                        t = V.do(lambda e: e.tensor_tensor(
                            ST[:, :, :], ST[:, :, :], EL[:, c, :].unsqueeze(2).to_broadcast([128, 8, 64]), ALU.mult),
                            to, r["el"])
                        t = V.do(lambda e: e.tensor_tensor(ST[:, :, :], ST[:, :, :], bsv, ALU.add), t, ts)
                    bs.rel = [t]
                    prev["st"] = t
                else:
                    prev["sto"] = to
                yield
                fns = []
                for h in range(8):
                    q, o = h // 2, 64 * (h % 2)
                    fns.append(lambda e, h=h, q=q, o=o: e.matmul(
                        bd.ap[o:o + 64, 128 * q:128 * q + 128], xd[:, h, :], E[:, h, :], start=True, stop=True))
                td = PE.many(fns, r["m"], r["xd"], bd.take())
                prev["e"] = td
                prev[("xd", c % 2)] = td
                yield
                bdv = bd.ap[:, :].rearrange("p (q t) -> p q t", q=4)
                if c > 0:
                    t = V.do(lambda e: e.tensor_tensor(YT[:, :, :], bdv, YT[:, :, :], ALU.add), tyo, td)
                    bd.rel = [t]
                    yv = YT
                else:
                    t, yv = td, bdv
                for q in range(4):
                    tt = V.do(lambda e, q=q, yv=yv: e.scalar_tensor_tensor(
                        xs[:, q, cs], xs[:, q, cs], cv[:, VOFF["m_d"][0] + 4 * g + q:VOFF["m_d"][0] + 4 * g + q + 1],
                        yv[:, q, :], ALU.mult, ALU.add), t)
                if c == 0:
                    bd.rel = [tt]
                return tt

            for c in range(4):
                r = yield from prep(c)
                yield
                if c in (1, 2):
                    loads[c + 1] = load(c + 1)
                tt = yield from finish(c, r)
                yield
            bc_rel[p] = [PE.last()]
            done = []
            for q in range(4):
                done.append(V.do(lambda e, q=q: e.scalar_tensor_tensor(
                    Y[:, 4 * g + q, :], xs[:, q, :], 0.5, Y[:, 4 * g + q, :], ALU.mult, ALU.mult), tt, y_t[g][q]))
            xs_rel[p] = [done[-1]]
            ss = SumSq(4)
            for q in range(4):
                ss.add(Y[:, 4 * g + q, :], done[q])
                yield
            yield
            t = ss.sum(aux[2])
            yield
            lnexp()
            rt = rsqrt(aux[2], 512, R[:, :], t, V.last())
            exptanh()
            yield
            for q in range(4):
                n = 4 * g + q
                done[q] = V.do(lambda e, n=n: e.scalar_tensor_tensor(
                    Y[:, n, :], Y[:, n, :], cv[:, VOFF["m_norm_g"][0] + n:VOFF["m_norm_g"][0] + n + 1], R[:, :],
                    ALU.mult, ALU.mult), rt)
            ssd_done[g] = done
            yield

        def weave(*gens):
            live = [[g, n, 0] for g, n in gens]
            while live:
                g = min(live, key=lambda x: x[2] / x[1])
                g[2] += 1
                try:
                    next(g[0])
                except StopIteration:
                    live.remove(g)

        weave((in_proj(0), 80), (chain(*[ada_piece(ada_next) for _ in range(2)]), 16))
        for g in range(1, 4):
            weave((in_proj(g), 80), (ssd(g - 1), 33), (chain(*[ada_piece(ada_next) for _ in range(2)]), 16))

        def split_act(src, hi, lo, t, free, eng=None):
            th = A.do(lambda e: e.activation(hi, src, ACT.Copy), t, free)
            tl = (G.do if eng is G else V.later)(lambda e: e.tensor_tensor(lo, src, hi.bitcast(F32), ALU.subtract), t, th, free)
            return [th, tl]

        xt = [t_x] * NB

        def residual(bank, t, k, gcol):
            if gcol is None:
                r = V.do(lambda e: e.tensor_tensor(X[:, k, :], bank.ap[:, :], X[:, k, :], ALU.add), t, xt[k])
            else:
                r = V.do(lambda e: e.scalar_tensor_tensor(X[:, k, :], bank.ap[:, :], ada[:, gcol + k:gcol + k + 1],
                                                          X[:, k, :], ALU.mult, ALU.add), t, xt[k])
            bank.rel = [r]
            xt[k] = r
            return r

        h_rel = [PE.last(), PE.last()]
        sx = SumSq(NB)

        def out_proj(g):
            o = 4 * (g % 2)
            marks = [None] * 8
            for q in range(4):
                marks[o + q] = split_act(Y[:, 4 * g + q, :], HH[:, o + q, :], HL[:, o + q, :], ssd_done[g][q],
                                         h_rel[g % 2], G if q % 2 else V)
            yield
            for i2 in range(2):
                i = use("out")
                for j in range(4):
                    n = 4 * i2 + j
                    bank = dense.next()
                    t = yield from gblock(i, j, 512, H, marks, bank, kb0=o)
                    residual(bank, t, n, 16)
                    if g == 3:
                        sx.add(X[:, n, :], xt[n])
                    yield
            h_rel[g % 2] = PE.last()

        weave((chain(out_proj(0), out_proj(1)), 66), (ssd(3), 33), (chain(*[ada_piece(ada_next) for _ in range(2)]), 16))
        weave((chain(out_proj(2), out_proj(3)), 66), (chain(*[ada_piece(ada_next) for _ in range(2)]), 30))
        lnexp()

        t_fence = fence()
        ph.close()
        ph = ExitStack()
        KT = psb("KT", [128, NB, S])
        VT = psb("VT", [128, 4, D])
        QT = psb("QT", [128, NB, S])
        OZ = psb("OZ", [128, NB, S])
        W = psb("W", [128, 12, S])
        ATr = Ring([Slot(psb(f"AT{i}", [128, 4, 128])) for i in range(3)])
        wslots = [Slot(W[:, 4 * n:4 * n + 4, :].rearrange("p a b -> p (a b)")) for n in range(3)]
        s_w = [sem(f"s_w{n}") for n in range(3)]
        for n in range(3):
            ada_load(wslots[n], s_w[n], 1, t_fence)

        def ada_more(count):
            for _ in range(count):
                i = ada_at["use"]
                n = (i - 20) % 3
                yield from ada_piece(lambda: ada_at["load"] < 32 and ada_load(wslots[n], s_w[n], (i - 20) // 3 + 2), aux[4])

        t = sx.sum(aux[0])
        rt = rsqrt(aux[0], D, R[:, :], t, V.last())
        tg = gain(G1[:, 8:16], vcol("kv_norm_g"), ada[:, 32:40], V.last())
        V.wait(tg)
        ht = modulated(G1[:, 8:16], ada[:, 24:32], PE.last(), xt, rt)
        kt, vt = {}, []

        def kv_proj():
            for i4 in range(4):
                i = use("kv")
                bks = [dense.next(), dense.next()]
                if i4 == 0:
                    t = yield from gblocks(i, (0, 1), 256, H, ht, bks)
                for j in range(2):
                    bank = bks[j]
                    if i4:
                        t = yield from gblock(i, j, 256, H, ht, bank)
                    n = 2 * i4 + j
                    kt[n] = A.do(lambda e, n=n, bank=bank: e.activation(KT[:, n, :], bank.ap[:, :], ACT.Copy), t)
                    bank.rel = [kt[n]]
                    yield
            for i4 in range(4):
                i = use("kv")
                for pr in range(2):
                    bank = dense.next()
                    block_tok(i, 2 * pr, 256, H, ht[:], bank, 0, True)
                    yield
                    t = block_tok(i, 2 * pr + 1, 256, H, ht[:], bank, 1, False)
                    t = A.do(lambda e, pr=pr, i4=i4, bank=bank: e.activation(
                        VT[:, 2 * pr:2 * pr + 2, 256 * i4:256 * i4 + 256],
                        bank.ap[:, :].rearrange("p (a n) -> p a n", a=2), ACT.Copy), t)
                    bank.rel = [t]
                    vt.append(t)
                    yield

        weave((kv_proj(), 76), (ada_more(12), 92))
        tg = gain(G1[:, 16:24], cv[:, VOFF["norm_g"][0] + 8:VOFF["norm_g"][0] + 16], ada[:, 48:56], V.last())
        V.wait(tg)
        ht = modulated(G1[:, 16:24], ada[:, 40:48], PE.last(), xt, rt)
        qt, zt = {}, {}

        gated = {}

        def gate_o(n):
            if n in osb and n in zt:
                gated[n] = V.do(lambda e: e.scalar_tensor_tensor(
                    OZ[:, n, :], QT[:, n, :], 0.5, OZ[:, n, :], ALU.mult, ALU.mult), zt[n], osb[n])

        def sb_proj():
            for i4 in range(4):
                i = use("q")
                bks = [dense.next(), dense.next()]
                if i4 == 0:
                    t = blocks(i, (0, 1), 256, H, ht, bks)
                for j in range(2):
                    bank = bks[j]
                    if i4:
                        t = yield from gblock(i, j, 256, H, ht, bank)
                    n = 2 * i4 + j
                    qt[n] = A.do(lambda e, n=n, bank=bank: e.activation(QT[:, n, :], bank.ap[:, :], ACT.Copy, scale=0.125), t)
                    bank.rel = [qt[n]]
                    yield
            for i4 in range(4):
                i = use("sz")
                pend = []
                for j in range(2):
                    bank = dense.next()
                    pend.append((bank, (yield from gblock(i, j, 256, H, ht, bank))))
                    if j == 0:
                        yield
                exptanh()
                for j in range(2):
                    n = 2 * i4 + j
                    zt[n] = twice_silu(pend[j][0], pend[j][1], OZ[:, n, :], None)
                lnexp()
                for j in range(2):
                    gate_o(2 * i4 + j)
                yield

        zbanks = Ring(aux[0:2])
        tbanks = Ring(aux[2:4])
        osb = {}

        def attend_unit(h, tb):
            n, o = h // 2, 64 * (h % 2)
            hi = 128 * (tb + 1)
            bz = zbanks.next()
            z = bz.ap[:, 0:hi]
            tz = PE.do(lambda e: e.matmul(z, QT[o:o + 64, n, 128 * tb:128 * tb + 128], KT[o:o + 64, n, 0:hi],
                                          start=True, stop=True), qt[n], kt[n], bz.take())
            a, zc = aring.next(), zring.next()
            av, zv = a.ap[:, 0:hi], zc.ap[:, 0:hi]
            yield
            tz = V.do(lambda e: e.tensor_copy(zv, z), tz, zc.take())
            bz.rel = [tz]
            t = V.do(lambda e: e.tensor_scalar(av, zv, 30.0, None, ALU.min), tz, a.take())
            yield
            t = A.do(lambda e: e.activation(av, av, ACT.Exp), t)
            t = A.do(lambda e: e.activation(av, av, ACT.Ln, bias=1.0), t)
            yield
            t = V.do(lambda e: e.tensor_tensor(av, zv, av, ALU.max), t)
            t = V.do(lambda e: e.tensor_tensor_scan(av[:, ::-1], smask[:, S - hi:S][:, ::-1], av[:, ::-1], 0.0,
                                                    ALU.mult, ALU.add), t)
            t = V.do(lambda e: e.tensor_tensor(av, zv, av, ALU.subtract), t)
            zc.rel = [t]
            yield
            ta = A.do(lambda e: e.activation(av, av, ACT.Exp), t)
            t = G.do(lambda e: e.tensor_tensor(av[:, hi - 128:hi], av[:, hi - 128:hi], amask, ALU.mult), ta)
            yield
            yield
            bt = tbanks.next()
            tt = PE.many([lambda e, s=s: e.transpose(bt.ap[:, 128 * s:128 * s + 128], av[:, 128 * s:128 * s + 128], ident)
                          for s in range(tb + 1)], ta, t, bt.take())
            a.rel = [tt]
            at = ATr.next()
            tc = A.do(lambda e: e.activation(at.ap[:, 0:tb + 1, :], bt.ap[:, 0:hi].rearrange("p (s t) -> p s t", t=128),
                                             ACT.Copy), tt, at.take())
            bt.rel = [tc]
            yield
            ob = aux[4]
            free = ob.take() if (o == 0 and tb == 0) else None
            tp = PE.many([lambda e, s=s: e.matmul(
                ob.ap[o:o + 64, 128 * tb:128 * tb + 128], VT[:, s, 64 * h:64 * h + 64], at.ap[:, s, :],
                start=(s == 0), stop=(s == tb)) for s in range(tb + 1)], tc, vt, free)
            at.rel = [tp]
            if o == 64 and tb == 3:
                t = A.do(lambda e: e.activation(QT[:, n, :], ob.ap[:, :], ACT.Copy), tp)
                ob.rel = [t]
                osb[n] = t
                gate_o(n)

        def pipelined(units, depth):
            units = list(units)
            live = []
            k = 0
            while units or live:
                for g in list(live):
                    try:
                        next(g)
                    except StopIteration:
                        live.remove(g)
                if units and len(live) < depth:
                    g = units.pop(0)
                    live.append(g)
                    next(g)
                yield

        aring = Ring([Slot(W[:, n, :]) for n in range(7)])
        zring = Ring([Slot(W[:, 7 + n, :]) for n in range(5)])
        for q in aring.slots + zring.slots:
            q.rel = [PE.last(), V.last()]
        proj = sb_proj()
        for _ in range(2):
            next(proj)
        weave((pipelined([attend_unit(h, tb) for h in range(16) for tb in range(4)], 8), 72), (proj, 112))
        exptanh()
        marks = []
        hfree = PE.last()
        for n in range(NB):
            marks.append(split_act(OZ[:, n, :], HH[:, n, :], HL[:, n, :], gated[n], hfree, G if n % 2 else V))
        s1, s2 = SumSq(NB), SumSq(NB, acc=R)
        gm = V.do(lambda e: e.tensor_tensor(G1[:, 24:32], vcol("final_g"), vcol("mix_g"), ALU.mult), t_vec)
        for i4 in range(4):
            i = use("so")
            bks = [dense.next(), dense.next()]
            if i4 == 0:
                t = blocks(i, (0, 1), 256, H, marks, bks)
            for j in range(2):
                n = 2 * i4 + j
                if i4:
                    t = block(i, j, 256, H, marks, bks[j])
                residual(bks[j], t, n, 56)
                s1.add(X[:, n, :], xt[n])
                s2.add(X[:, n, :], xt[n], vcol("final_g")[:, n:n + 1])
        lnexp()

        r1, r2 = Slot(SQ), tmpr.next()
        t = s1.sum(aux[0])
        t2 = s2.sum(aux[1])
        t = rt1 = rsqrt(aux[0], D, r1.ap[:, :], t, r1.take())
        t = V.do(lambda e: e.tensor_tensor(r2.ap[:, :], r1.ap[:, :], r1.ap[:, :], ALU.mult), t, r2.take())
        t = V.do(lambda e: e.tensor_tensor(r2.ap[:, :], aux[1].ap[:, :], r2.ap[:, :], ALU.mult), t, t2)
        aux[1].rel = [t]
        t = A.do(lambda e: e.activation(r2.ap[:, :], r2.ap[:, :], ACT.Ln, scale=1.0 / D, bias=eps_ap), t)
        t = A.do(lambda e: e.activation(r2.ap[:, :], r2.ap[:, :], ACT.Exp, scale=-0.5), t)
        rt = V.do(lambda e: e.tensor_tensor(R[:, :], r1.ap[:, :], r2.ap[:, :], ALU.mult), t, t2)
        r2.rel = [rt]
        V.wait(gm)
        ht = modulated(G1[:, 24:32], None, PE.last(), xt, rt)
        fg = vcol("final_g")
        for k in range(NB):
            xt[k] = V.do(lambda e, k=k: e.scalar_tensor_tensor(X[:, k, :], X[:, k, :], fg[:, k:k + 1], r1.ap[:, :],
                                                          ALU.mult, ALU.mult), xt[k])
        r1.rel = [xt[NB - 1]]

        fence()
        ph.close()
        ph = ExitStack()
        OA = psb("OA", [128, 2, 4, S], F32R)
        QB = psb("QB", [128, 4, S])
        KB = psb("KB", [128, 4, S])
        VB = psb("VB", [128, 4, 512])
        ph2 = ExitStack()
        psb2 = lambda n, shape, dt=F32: sbt(n, shape, dt, ph2)
        HQ = psb2("HQ", [128, 4, S])
        HK = psb2("HK", [128, 4, S])
        HT = [psb2("HT0", [128, 4 * S]), psb2("HT1", [128, 2 * S])]
        HI = psb2("HI", [128, 4, 512])
        GG = psb2("GG", [128, 4, S])
        AD = psb2("AD", [128, 4, 4, 128])
        lbt = psb2("lbt", [128, 12])

        lg = vcol("lb")
        t = V.do(lambda e: e.tensor_tensor(lbt[:, 0:4], lg, lg, ALU.subtract), t_vec)
        t = A.do(lambda e: e.activation(lbt[:, 0:4], lbt[:, 0:4], ACT.Exp), t)
        t = V.do(lambda e: e.reciprocal(lbt[:, 4:8], lbt[:, 0:4]), t)
        t = V.do(lambda e: e.tensor_tensor(lbt[:, 0:4], lbt[:, 0:4], lbt[:, 4:8], ALU.mult), t)
        t = V.do(lambda e: e.tensor_tensor(lbt[:, 4:8], lbt[:, 0:4], lbt[:, 0:4], ALU.subtract), t)
        t_lb = V.do(lambda e: e.tensor_scalar(lbt[:, 8:12], lbt[:, 4:8], -1.0, 1.0, ALU.mult, ALU.add), t)

        hq, hk, hf, hg, hi_ = {}, {}, {}, {}, []
        for i2 in range(2):
            i = use("in2")
            bks = [dense.next(), dense.next()]
            if i2 == 0:
                t = blocks(i, (0, 1), 256, H, ht, bks)
            for j in range(2):
                n = 2 * i2 + j
                bank = bks[j]
                if i2:
                    t = block(i, j, 256, H, ht, bank)
                hq[n] = A.do(lambda e, n=n, bank=bank: e.activation(HQ[:, n, :], bank.ap[:, :], ACT.Copy, scale=128 ** -0.5), t)
                bank.rel = [hq[n]]
        for i2 in range(2):
            i = use("in2")
            for j in range(2):
                n = 2 * i2 + j
                bank = dense.next()
                t = block(i, j, 256, H, ht, bank)
                fs = HT[0][:, S * n:S * n + S]
                ts = A.do(lambda e, bank=bank, fs=fs: e.activation(fs, bank.ap[:, :], ACT.Sigmoid), t)
                bank.rel = [ts]
                hf[n] = V.do(lambda e, fs=fs, n=n: e.tensor_scalar(fs, fs, lbt[:, 8 + n:9 + n], lbt[:, 4 + n:5 + n],
                                                                   ALU.mult, ALU.add), ts, t_lb)
                hk[n] = V.do(lambda e, fs=fs, n=n: e.tensor_scalar(HK[:, n, :], fs, -1.0, 1.0, ALU.mult, ALU.add),
                             hf[n])
        hqk = [hq[3], hk[3], hf[3]]
        offt = {}

        def hgrn():
            sb2 = Ring(aux[0:2])
            ready = list(hqk)
            ad_t = [None] * 4
            used = None
            for lv in range(8):
                m = 0 if lv == 0 else 1 << (lv - 1)
                for tb in range(4):
                    bank = sb2.next()
                    cs = slice(128 * tb, 128 * tb + 128)
                    t = PE.many([lambda e, h=h, bank=bank, cs=cs: e.matmul(
                        bank.ap[:, 128 * h:128 * h + 128], HK[:, h, cs], HQ[:, h, cs], start=True, stop=True)
                        for h in range(4)], ready, bank.take())
                    bv = bank.ap[:, :].rearrange("p (h t) -> p h t", h=4)
                    if lv == 0:
                        ad_t[tb] = V.do(lambda e, bv=bv, tb=tb: e.tensor_tensor(
                            AD[:, tb, :, :], bv, ident.unsqueeze(1).to_broadcast([128, 4, 128]), ALU.mult), t)
                    else:
                        ad_t[tb] = V.do(lambda e, bv=bv, tb=tb, lv=lv: e.copy_predicated(
                            AD[:, tb, :, :], mk[:, lv - 1, :].unsqueeze(1).to_broadcast([128, 4, 128]), bv),
                            t, ad_t[tb], t_mk)
                    bank.rel = [ad_t[tb]]
                    yield
                used = PE.last()
                ready = grow(m, used, ready)
                yield
            return

        tcur = [0]

        def grow(m, used, ready):
            q, k = HQ[:, :, :].rearrange("p h t -> p (h t)"), HK[:, :, :].rearrange("p h t -> p (h t)")
            if m == 0:
                t = V.do(lambda e: e.tensor_tensor(q, q, HT[0][:, :], ALU.mult), used, ready)
                return [t]
            nb = 4 * S // (2 * m)
            tt = HT[tcur[0]][:, 0:2 * nb].rearrange("p (b two) -> p b two", two=2)
            q4 = q.rearrange("p (b two m) -> p b two m", two=2, m=m)
            k4 = k.rearrange("p (b two m) -> p b two m", two=2, m=m)
            nxt = HT[1 - tcur[0]][:, 0:nb]
            tcur[0] = 1 - tcur[0]
            t1 = V.do(lambda e: e.tensor_tensor(
                q4[:, :, 1, :], q4[:, :, 1, :], tt[:, :, 0].unsqueeze(2).to_broadcast([128, nb, m]), ALU.mult),
                used, ready)
            t2 = V.do(lambda e: e.tensor_tensor(
                k4[:, :, 0, :], k4[:, :, 0, :], tt[:, :, 1].unsqueeze(2).to_broadcast([128, nb, m]), ALU.mult))
            if m == 128:
                return [t1, t2]
            t3 = V.do(lambda e: e.tensor_tensor(nxt, tt[:, :, 0], tt[:, :, 1], ALU.mult))
            return [t1, t2, t3]

        qbt, kbt, vbt = {}, {}, []

        def head_norm(src, n, mark, gname):
            ss = SumSq(1, onesm=bones)
            ss.add(src[:, n, :], mark)
            b = aux[2 + n % 2]
            t = ss.sum(b)
            r = tmpr.next()
            rt = rsqrt(b, 64, r.ap[:, :], t, r.take())
            t = V.do(lambda e: e.scalar_tensor_tensor(src[:, n, :], src[:, n, :], vcol(gname), r.ap[:, :],
                                                      ALU.mult, ALU.mult), rt, t)
            r.rel = [t]
            return t

        def in2_rest():
            for i2 in range(2):
                i = use("in2")
                for pr in range(2):
                    bank = dense.next()
                    block_tok(i, 2 * pr, 256, H, ht[:], bank, 0, True)
                    yield
                    t = block_tok(i, 2 * pr + 1, 256, H, ht[:], bank, 1, False)
                    t = A.do(lambda e, bank=bank, pr=pr, i2=i2: e.activation(
                        HI[:, 2 * pr:2 * pr + 2, 256 * i2:256 * i2 + 256],
                        bank.ap[:, :].rearrange("p (a n) -> p a n", a=2), ACT.Copy), t)
                    bank.rel = [t]
                    hi_.append(t)
                    yield
            for i2 in range(2):
                i = use("in2")
                for j in range(2):
                    bank = dense.next()
                    t = yield from gblock(i, j, 256, H, ht, bank)
                    n = 2 * i2 + j
                    hg[n] = twice_silu(bank, t, GG[:, n, :], None)
                    yield
            lnexp()
            for dst, marks, gname in ((QB, qbt, "qn"), (KB, kbt, "kn")):
                for i2 in range(2):
                    i = use("in2")
                    for j in range(2):
                        bank = dense.next()
                        t = yield from gblock(i, j, 256, H, ht, bank)
                        n = 2 * i2 + j
                        marks[n] = A.do(lambda e, bank=bank, n=n, dst=dst: e.activation(
                            dst[:, n, :], bank.ap[:, :], ACT.Copy), t)
                        bank.rel = [marks[n]]
                        marks[n] = head_norm(dst, n, marks[n], gname)
                        yield
            for i2 in range(2):
                i = use("in2")
                for pr in range(2):
                    bank = dense.next()
                    block_tok(i, 2 * pr, 256, H, ht[:], bank, 0, True)
                    yield
                    t = block_tok(i, 2 * pr + 1, 256, H, ht[:], bank, 1, False)
                    t = A.do(lambda e, bank=bank, pr=pr, i2=i2: e.activation(
                        VB[:, 2 * pr:2 * pr + 2, 256 * i2:256 * i2 + 256],
                        bank.ap[:, :].rearrange("p (a n) -> p a n", a=2), ACT.Copy), t)
                    bank.rel = [t]
                    vbt.append(t)
                    yield

        def hgrn_rest():
            ready = []
            off = {}
            sb2 = Ring(aux[0:2])
            for m, pairs in ((128, ((0, 1), (2, 3))), (256, ((0, 2), (1, 2), (0, 3), (1, 3)))):
                if m == 256:
                    grow(128, PE.last(), V.last())
                    ready = V.last()
                    yield
                for s, tb in pairs:
                    bank = sb2.next()
                    t = PE.many([lambda e, h=h, bank=bank, s=s, tb=tb: e.matmul(
                        bank.ap[:, 128 * h:128 * h + 128], HK[:, h, 128 * s:128 * s + 128],
                        HQ[:, h, 128 * tb:128 * tb + 128], start=True, stop=True) for h in range(4)],
                        V.last(), bank.take())
                    o = OFF[len(off)]
                    ta = A.do(lambda e, bank=bank, o=o: e.activation(
                        o[:, :, :], bank.ap[:, :].rearrange("p (h t) -> p h t", h=4), ACT.Copy), t)
                    bank.rel = [ta]
                    off[(s, tb)] = (o, ta)
                    yield
            for tb in range(4):
                bank = sb2.next()
                fns = []
                for h in range(4):
                    for s in range(tb + 1):
                        a = AD[:, tb, h, :] if s == tb else off[(s, tb)][0][:, h, :]
                        fns.append(lambda e, h=h, s=s, a=a, bank=bank, tb=tb: e.matmul(
                            bank.ap[:, 128 * h:128 * h + 128], HI[:, s, 128 * h:128 * h + 128], a,
                            start=(s == 0), stop=(s == tb)))
                t = PE.many(fns, V.last(), A.last(), hi_, bank.take())
                ta = A.do(lambda e, bank=bank, tb=tb: e.activation(
                    HQ[:, :, 128 * tb:128 * tb + 128], bank.ap[:, :].rearrange("p (h t) -> p h t", h=4), ACT.Copy), t)
                bank.rel = [ta]
                yield
            lnexp()
            for h in range(4):
                b = aux[h % 2]
                ss = SumSq(1)
                ss.add(HQ[:, h, :], ta)
                t = ss.sum(b)
                r = tmpr.next()
                rt = rsqrt(b, 128, r.ap[:, :], t, r.take())
                t = V.do(lambda e, h=h, r=r: e.scalar_tensor_tensor(HQ[:, h, :], HQ[:, h, :], vcol("onorm"), r.ap[:, :],
                                                                    ALU.mult, ALU.mult), rt)
                r.rel = [t]
                t = V.do(lambda e, h=h: e.scalar_tensor_tensor(GG[:, h, :], HQ[:, h, :], 0.5, GG[:, h, :],
                                                               ALU.mult, ALU.mult), t, hg[h])
                oat.append(split_act(GG[:, h, :], OA[:, 0, h, :], OA[:, 1, h, :], t, None))
                yield

        oat = []
        OFF = [psb2("OFF", [128, 4, 128])] + [
            b[:, 512 * k:512 * k + 512].rearrange("p (h t) -> p h t", h=4)
            for b, k in ((HT[0], 0), (HT[0], 1), (HT[0], 2), (HT[0], 3), (HT[1], 1))]
        weave((chain(hgrn(), hgrn_rest()), 60), (in2_rest(), 115))

        fence()
        ph2.close()
        ph2 = ExitStack()
        BW = Ring([Slot(psb2(f"BW{i}", [128, S])) for i in range(2)])
        PS = Ring([Slot(psb2(f"PS{i}", [128, S])) for i in range(3)])
        PT = Ring([Slot(psb2(f"PT{i}", [128, 4, 128])) for i in range(2)])
        OB = psb2("OB", [128, 2, 4, S], F32R)
        SGA = psb2("SGA", [128, 8, S])
        SGB = psb2("SGB", [128, 4, S])
        sm = Ring([Slot(psb2(f"sm{i}", [128, 4])) for i in range(4)])
        s_bw = [sem("s_bw0"), sem("s_bw1")]
        bw = {}

        def load_bias(h):
            b = BW.next()
            t = SP.dma(lambda e: e.dma_start(b.ap[:, :], rbx[h]), s_bw[h % 2], h // 2 + 1, b.take(), t_fence)
            t = G.do(lambda e: e.memset(b.ap[0:64, 448:512], -1e30), t)
            bw[h] = (b, t)

        t_fence = [q.last() for q in (V, A, G, PE)]

        def band_unit(h, tb):
            n, o = h // 2, 64 * (h % 2)
            hi = 128 * (tb + 1)
            bz = zbanks.next()
            z = bz.ap[:, 0:hi]
            tz = PE.do(lambda e: e.matmul(z, QB[o:o + 64, n, 128 * tb:128 * tb + 128], KB[o:o + 64, n, 0:hi],
                                          start=True, stop=True), qbt[n], kbt[n], bz.take())
            a, m = PS.next(), sm.next()
            av = a.ap[:, 0:hi]
            if tb == 0:
                if h == 0:
                    load_bias(0)
                if h + 1 < 8:
                    load_bias(h + 1)
            b, tb_ = bw[h]
            t = V.do(lambda e: e.scalar_tensor_tensor(av, z, 0.125, b.ap[:, S - hi:S], ALU.mult, ALU.add),
                     tz, tb_, a.take())
            bz.rel = [t]
            if tb == 3:
                b.rel = [t]
            t = V.do(lambda e, m=m: e.tensor_reduce(m.ap[:, 0:1], av, AX, ALU.max), t, m.take())
            t = V.do(lambda e, m=m: e.tensor_scalar(m.ap[:, 1:2], m.ap[:, 0:1], -1.0, None, ALU.mult), t)
            t = A.do(lambda e, m=m: e.activation(av, av, ACT.Exp, bias=m.ap[:, 1:2], accum_out=m.ap[:, 2:3]), t)
            yield
            t = V.do(lambda e, m=m: e.reciprocal(m.ap[:, 3:4], m.ap[:, 2:3]), t)
            t = V.do(lambda e, m=m: e.tensor_scalar(av, av, m.ap[:, 3:4], None, ALU.mult), t)
            m.rel = [t]
            yield
            bt = tbanks.next()
            tt = PE.many([lambda e, s=s: e.transpose(bt.ap[:, 128 * s:128 * s + 128], av[:, 128 * s:128 * s + 128], ident)
                          for s in range(tb + 1)], t, bt.take())
            a.rel = [tt]
            at = PT.next()
            tc = A.do(lambda e: e.activation(at.ap[:, 0:tb + 1, :], bt.ap[:, 0:hi].rearrange("p (s t) -> p s t", t=128),
                                             ACT.Copy), tt, at.take())
            bt.rel = [tc]
            yield
            ob = aux[4]
            free = ob.take() if (o == 0 and tb == 0) else None
            tp = PE.many([lambda e, s=s: e.matmul(
                ob.ap[o:o + 64, 128 * tb:128 * tb + 128], VB[:, s, 64 * h:64 * h + 64], at.ap[:, s, :],
                start=(s == 0), stop=(s == tb)) for s in range(tb + 1)], tc, vbt, free)
            at.rel = [tp]
            if o == 64 and tb == 3:
                q = tmpr.next()
                t = A.do(lambda e: e.activation(q.ap[:, :], ob.ap[:, :], ACT.Copy), tp, q.take())
                ob.rel = [t]
                m = split_act(q.ap[:, :], OB[:, 0, n, :], OB[:, 1, n, :], t, None)
                q.rel = list(m)
                obt.append(m)

        obt = []
        sga = {}

        def gate(i, j, dst, free):
            bank = dense.next()
            t = yield from gblock(i, j, 256, H, ht, bank)
            t = A.do(lambda e: e.activation(dst, bank.ap[:, :], ACT.Tanh, scale=0.5), t, free)
            bank.rel = [t]
            return t

        def gates_a():
            for i4 in range(4):
                i = use("in2")
                for j in range(2):
                    n = 2 * i4 + j
                    sga[n] = yield from gate(i, j, SGA[:, n, :], None)
                    yield

        def branch_a():
            for i2 in range(2):
                i = use("wa")
                for j in range(4):
                    n = 4 * i2 + j
                    bank = dense.next()
                    t = block(i, j, 512, (OA[:, 0, :, :], OA[:, 1, :, :]), oat, bank)
                    sga[n] = V.do(lambda e, n=n, bank=bank: e.scalar_tensor_tensor(
                        SGA[:, n, :], SGA[:, n, :], 1.0, bank.ap[:, :], ALU.add, ALU.mult), t, sga[n])
                    bank.rel = [sga[n]]
                    yield

        exptanh()
        weave((pipelined([band_unit(h, tb) for h in range(8) for tb in range(4)], 4), 36), (chain(gates_a(), branch_a()), 96))

        sgb_free = [None] * 4
        for i2 in range(2):
            tg = []
            for c in range(2):
                i = use("in2")
                for j in range(2):
                    tg.append(run(gate(i, j, SGB[:, 2 * c + j, :], sgb_free[2 * c + j])))
            i = use("wb")
            for j in range(4):
                n = 4 * i2 + j
                bank = dense.next()
                t = block(i, j, 512, (OB[:, 0, :, :], OB[:, 1, :, :]), obt, bank)
                t = V.do(lambda e, j=j, bank=bank: e.scalar_tensor_tensor(
                    SGB[:, j, :], SGB[:, j, :], 1.0, bank.ap[:, :], ALU.add, ALU.mult), t, tg[j])
                bank.rel = [t]
                sga[n] = V.do(lambda e, n=n, j=j: e.tensor_tensor(SGA[:, n, :], SGB[:, j, :], SGA[:, n, :], ALU.add), t, sga[n])
                sgb_free[j] = sga[n]
        hfree = PE.last()
        marks = []
        for n in range(NB):
            t = V.do(lambda e, n=n: e.tensor_scalar(SGA[:, n, :], SGA[:, n, :], 0.5, None, ALU.mult), sga[n])
            marks.append(split_act(SGA[:, n, :], HH[:, n, :], HL[:, n, :], t, hfree, G if n % 2 else V))
        lnexp()
        sx = SumSq(NB)
        for i4 in range(4):
            i = use("wo2")
            bks = [dense.next(), dense.next()]
            if i4 == 0:
                t = blocks(i, (0, 1), 256, H, marks, bks)
            for j in range(2):
                n = 2 * i4 + j
                if i4:
                    t = block(i, j, 256, H, marks, bks[j])
                residual(bks[j], t, n, None)
                sx.add(X[:, n, :], xt[n])

        t = sx.sum(aux[0])
        rt = rsqrt(aux[0], D, R[:, :], t, V.last())
        ht = modulated(vcol("ffn_g"), None, PE.last(), xt, rt)
        exptanh()
        fence()
        ph2.close()
        ph.close()
        ph = ExitStack()
        FH = psb("FH", [128, 22, S], F32R)
        FL = psb("FL", [128, 22, S], F32R)
        pstage = [psb(f"pst{i}", [128, S]) for i in range(3)]
        ft = []
        for i11 in range(11):
            ig = use("fg")
            bg = []
            bks = [dense.next(), dense.next()]
            if i11 == 0:
                t = blocks(ig, (0, 1), 256, H, ht, bks)
            for j in range(2):
                if i11:
                    t = block(ig, j, 256, H, ht, bks[j])
                q = tmpr.next()
                bg.append((q, twice_silu_into(q, bks[j], t)))
            iu = use("fu")
            for j in range(2):
                n = 2 * i11 + j
                bank = dense.next()
                t = block(iu, j, 256, H, ht, bank)
                q, tq = bg[j]
                t = V.do(lambda e, q=q, bank=bank: e.scalar_tensor_tensor(q.ap[:, :], q.ap[:, :], 0.5, bank.ap[:, :],
                                                                          ALU.mult, ALU.mult), t, tq)
                bank.rel = [t]
                m = split_act(q.ap[:, :], FH[:, n, :], FL[:, n, :], t, None, G if n % 2 else V)
                q.rel = list(m)
                ft.append(m)
        lnexp()
        hfree = PE.last()
        pq = [tmpr.next(), tmpr.next()]
        pm = {}
        for k in range(2):
            t = SP.dma(lambda e, k=k: e.dma_start(pq[k].ap[:, :], pT[:, k, :]), sem(f"s_p{k}"), 1, pq[k].take())
            pm[6 + k] = split_act(pq[k].ap[:, :], HH[:, 6 + k, :], HL[:, 6 + k, :], t, hfree)
            pq[k].rel = list(pm[6 + k])
        sx = SumSq(NB)
        for i4 in range(4):
            bk = [dense.next(), dense.next()]
            for c, (k0, kb) in enumerate(((0, 8), (8, 8), (16, 6))):
                i = use("fd")
                for j in range(2):
                    t = block(i, j, 256, (FH, FL), ft, bk[j], first=(c == 0), last=(c == 2), kb0=k0)
                    if c == 2:
                        n = 2 * i4 + j
                        residual(bk[j], t, n, None)
                        sx.add(X[:, n, :], xt[n])

        i = use("pp")
        s_pw = [sem(f"s_pw{n}") for n in range(3)]
        ppb = Ring([Slot(SP_) for SP_ in pstage])
        ppt = []
        for n in range(8):
            if n == 3:
                t = sx.sum(aux[0])
                rt = rsqrt(aux[0], D, R[:, :], t, V.last())
            bank = aux[1 + n % 4]
            t = block(i, n, 1024, (HH, HL), pm, bank, kb0=6)
            q = ppb.next()
            t = A.do(lambda e, q=q, bank=bank: e.activation(q.ap[:, :], bank.ap[:, :], ACT.Copy), t, q.take())
            bank.rel = [t]
            t = SP.dma(lambda e, n=n, q=q: e.dma_start(pscr[n], q.ap[:, :]), s_pw[n % 3], n // 3 + 1, t)
            q.rel = [t]
            ppt.append(t)
        ht = modulated(vcol("ple_g"), None, PE.last(), xt, rt)
        marks = fence()
        ph.close()
        ph = ExitStack()
        PP = psb("PP", [128, 8, S])
        ppl = [SP.dma(lambda e, n=n: e.dma_start(PP[:, n, :], pscr[n]), sem(f"s_pl{n}"), 1, marks, ppt) for n in range(8)]
        s_out = sem("s_out")
        for i4 in range(4):
            i = use("pg")
            for j in range(2):
                n = 2 * i4 + j
                bank = dense.next()
                t = block(i, j, 256, H, ht, bank)
                q = tmpr.next()
                ta = A.do(lambda e, q=q, bank=bank: e.activation(q.ap[:, :], bank.ap[:, :], ACT.Sigmoid), t, q.take())
                bank.rel = [ta]
                t = V.do(lambda e, q=q, n=n: e.tensor_tensor(q.ap[:, :], q.ap[:, :], PP[:, n, :], ALU.mult), ta, ppl[n])
                t = V.do(lambda e, q=q, n=n: e.tensor_tensor(X[:, n, :], X[:, n, :], q.ap[:, :], ALU.add), t, xt[n])
                q.rel = [t]
                SP.dma(lambda e, n=n: e.dma_start(out[128 * n:128 * n + 128, :], X[:, n, :]), s_out, n + 1, t)
        assert st["use"] == len(plan)
        SP.wait((s_out, 128))
        ph.close()

        blk = ctx.enter_context(nc.Block())

        @blk.sync
        def _(e):
            SP.play(e)

        @blk.tensor
        def _(e):
            PE.play(e)

        @blk.vector
        def _(e):
            V.play(e)

        @blk.scalar
        def _(e):
            A.play(e)

        @blk.gpsimd
        def _(e):
            G.play(e)


def columns(v):
    v = v.reshape(-1, 128)
    return v.T


def constants():
    i = np.arange(128)
    s, t = i[:, None], i[None, :]
    ident = (s == t).astype(np.float32)
    bones = ((s // 64) == (t // 64)).astype(np.float32)
    cmask = (s <= t).astype(np.float32)
    smask = (np.arange(512)[None, :] - 384 < s - 1).astype(np.float32)
    amask = (t < s).astype(np.float32)
    con = np.concatenate([ident, np.ones((128, 128), np.float32), bones, cmask, smask, amask], axis=1)
    masks = np.stack([((s // (2 * m)) == (t // (2 * m))) & ((s // m) % 2 == 0) & ((t // m) % 2 == 1)
                      for m in (1, 2, 4, 8, 16, 32, 64)], axis=1).astype(np.float32).reshape(128, 896)
    return np.ascontiguousarray(con), np.ascontiguousarray(masks)


def kernel(**inputs):
    import concourse.bacc as _bacc
    from concourse.bass_utils import run_bass_kernel_spmd as _run

    a = {k: np.asarray(v) for k, v in inputs.items()}
    parts = []
    for _, (name, k0, kb, cols) in weight_plan():
        w = a[name]
        if w.ndim == 3:
            w = w[0]
        w = w[128 * k0:128 * (k0 + kb)]
        w = np.concatenate([w[:, c:c + n] for c, n in cols], axis=1)
        parts.append(w.reshape(kb, 128, -1).transpose(1, 0, 2).reshape(-1))
    wstream = np.concatenate(parts)

    mod = [a["ada_w"][0], a["kv_ada_w"], a["ada_w"][1]]
    parts = [w.reshape(8, 128, -1, 256).transpose(2, 1, 0, 3).reshape(-1, 128, 2048) for w in mod]
    parts[0][0:8] = parts[0][[4, 0, 5, 1, 6, 2, 7, 3]]
    astream = np.concatenate(parts)

    first = np.zeros((2, 128), np.float32)
    first[0, 0:32] = a["m_dt_bias"][0]
    first[1, 0:32] = a["m_a_log"][0]
    vec = np.concatenate([
        columns(a["c"]), columns(a["ada_b"]), columns(a["norm_g"]), columns(a["m_conv_w"]),
        columns(a["m_conv_b"]), columns(np.repeat(a["m_d"][0], 64)), columns(a["m_norm_g"]),
        columns(a["kv_ada_b"]), columns(a["kv_norm_g"]), columns(a["final_g"]), columns(a["norm_mix_g_2"]),
        columns(a["hgrn_lb_logits_2"]), columns(a["hgrn_onorm_g_2"]),
        columns(np.tile(a["attn_qnorm_g_2"][0], 2)), columns(np.tile(a["attn_knorm_g_2"][0], 2)),
        columns(a["norm_ffn_g_2"]), columns(a["norm_ple_g_2"]), first.T], axis=1)
    con, masks = constants()
    xT = a["x"][0].T.reshape(8, 128, 512).transpose(1, 0, 2)
    pT = a["p_2"][0, 0].T.reshape(2, 128, 512).transpose(1, 0, 2)
    q, j = np.arange(128)[:, None], np.arange(512)[None, :]
    rbx = a["attn_rel_bias_2"][0][:, np.clip(q - j + 384, -128, 128) + 128]
    arrays = {"wstream": wstream, "astream": astream, "vec": vec, "con": con, "masks": masks, "xT": xT, "pT": pT, "rbx": rbx}
    arrays = {k: np.ascontiguousarray(v) for k, v in arrays.items()}

    nc = _bacc.Bacc("TRN2", target_bir_lowering=False, num_devices=1)
    aps = {k: nc.dram_tensor(k, v.shape, mybir.dt.from_np(v.dtype), kind="ExternalInput").ap()
           for k, v in arrays.items()}
    out = nc.dram_tensor("out", (1024, 512), F32, kind="ExternalOutput").ap()
    scratch = nc.dram_tensor("scratch", (32, 512), F32, kind="Internal").ap()
    pscr = nc.dram_tensor("pscr", (8, 128, 512), F32, kind="Internal").ap()
    program(nc, out=out, scratch=scratch, pscr=pscr, **aps)
    r = _run(nc, [arrays], core_ids=[0])
    return np.ascontiguousarray(r.results[0]["out"].T).reshape(1, 512, 1024)
```
